# Optimizing a Trainium2 kernel written in Bass

```python
import jax, jax.numpy as jnp
from jax import lax
import numpy as np

D_MODEL = 1024
BATCH = 1
SEQ = 512
DEPTH = 2

GRID_W = 64
CTX_LEN = 256
HEAD_DIM = 64
FNET_GROUPS = 8
FNET_WIDTH = FNET_GROUPS * HEAD_DIM
NA_HEADS = 8
NA_WIDTH = NA_HEADS * HEAD_DIM
NA_KR_MAX = 8
NA_KC = 16
NA_QB = 16
NA_KB = 32
GQA_Q_HEADS = 16
GQA_KV_HEADS = 4
GQA_WINDOW = 128
GQA_BLOCK = 128
ROPE_THETA = 10000.0
PEER_HEADS = 8
PEER_NKEYS = 128
PEER_EXPERTS = PEER_NKEYS * PEER_NKEYS
PEER_QDIM = 256
PEER_TOPK = 16
PEER_TOKEN_CHUNK = 128
N_EVEN = (DEPTH + 1) // 2
N_ODD = DEPTH // 2
DN_ALPHA = (2 * DEPTH) ** 0.25
DN_BETA = (8 * DEPTH) ** -0.25
LN_EPS = 1e-6
NEG = -1e30

kernel_name = "hybrid_fnet_natten_swa_peer_dit"

def _layer_norm(x, gain=None, bias=None):
    xf = x.astype(jnp.float32)
    mu = jnp.mean(xf, -1, keepdims=True)
    var = jnp.mean(jnp.square(xf - mu), -1, keepdims=True)
    y = (xf - mu) * lax.rsqrt(var + LN_EPS)
    if gain is not None:
        y = y * gain.astype(jnp.float32) + bias.astype(jnp.float32)
    return y.astype(x.dtype)

def _modulate(x, shift, scale):
    return _layer_norm(x) * (1 + scale) + shift

def _heads(t, n_heads):
    b, l, _ = t.shape
    return t.reshape(b, l, n_heads, HEAD_DIM)

def _axial_rope_tables(n_tokens):
    t = jnp.arange(n_tokens)
    row = (t // GRID_W).astype(jnp.float32)
    col = (t % GRID_W).astype(jnp.float32)
    n_freq = HEAD_DIM // 4
    inv_freq = ROPE_THETA ** (-jnp.arange(n_freq, dtype=jnp.float32) / n_freq)
    ang = jnp.concatenate([row[:, None] * inv_freq, col[:, None] * inv_freq], -1)
    return jnp.cos(ang), jnp.sin(ang)

def _apply_rope(x, cos, sin):
    x1, x2 = jnp.split(x.astype(jnp.float32), 2, axis=-1)
    cs = cos[None, :, None, :]
    sn = sin[None, :, None, :]
    return jnp.concatenate([x1 * cs - x2 * sn, x1 * sn + x2 * cs], -1).astype(x.dtype)

def _fourier_mix(u):
    b, l, _ = u.shape
    ug = u.astype(jnp.float32).reshape(b, l, FNET_GROUPS, HEAD_DIM)
    y = jnp.fft.fft2(ug, axes=(1, 3), norm="ortho").real
    return y.reshape(b, l, FNET_WIDTH).astype(u.dtype)

def _ctx_attention(q, k, v, sink=None):
    b, l, hq, dh = q.shape
    hkv = k.shape[2]
    g = hq // hkv
    qg = q.reshape(b, l, hkv, g, dh)
    s = jnp.einsum('bqhgd,bkhd->bhgqk', qg, k, preferred_element_type=jnp.float32) * (dh ** -0.5)
    if sink is not None:
        sk = jnp.broadcast_to(sink.reshape(hkv, g)[None, :, :, None, None].astype(jnp.float32), s.shape[:-1] + (1,))
        p = jax.nn.softmax(jnp.concatenate([s, sk], -1), -1)[..., :l]
    else:
        p = jax.nn.softmax(s, -1)
    o = jnp.einsum('bhgqk,bkhd->bqhgd', p.astype(v.dtype), v)
    return o.reshape(b, l, hq * dh)

def _neighbourhood_attention(q, k, v, k_ctx, v_ctx, rpb):
    b, s, h, dh = q.shape
    rows = s // GRID_W
    kr = min(NA_KR_MAX, rows)
    n_cb = GRID_W // NA_QB
    r = jnp.arange(rows)
    r_start = jnp.clip(r - kr // 2, 0, rows - kr)
    row_idx = r_start[:, None] + jnp.arange(kr)[None]
    c_start = jnp.clip(jnp.arange(GRID_W) - NA_KC // 2, 0, GRID_W - NA_KC)
    blk_start = jnp.clip(jnp.arange(n_cb) * NA_QB - NA_KC // 2, 0, GRID_W - NA_KB)
    blk_col = blk_start[:, None] + jnp.arange(NA_KB)[None]
    q_col = jnp.arange(n_cb)[:, None] * NA_QB + jnp.arange(NA_QB)[None]
    qc_start = c_start[q_col]
    kc = blk_col[:, None, :]
    valid = (kc >= qc_start[:, :, None]) & (kc < qc_start[:, :, None] + NA_KC)
    dr_i = row_idx - r[:, None] + (NA_KR_MAX - 1)
    dc_i = jnp.clip(kc - q_col[:, :, None], -(NA_KC - 1), NA_KC - 1) + (NA_KC - 1)
    bias = rpb[:, dr_i[:, None, None, :, None], dc_i[None, :, :, None, :]].astype(jnp.float32)

    scale = dh ** -0.5
    qg = q.reshape(b, rows, n_cb, NA_QB, h, dh)
    kg = k.reshape(b, rows, GRID_W, h, dh)
    vg = v.reshape(b, rows, GRID_W, h, dh)
    gi_r = row_idx[:, :, None, None]
    gi_c = blk_col[None, None, :, :]
    k_blk = kg[:, gi_r, gi_c]
    v_blk = vg[:, gi_r, gi_c]
    s_loc = jnp.einsum('brjqhd,brkjchd->bhrjqkc', qg, k_blk, preferred_element_type=jnp.float32) * scale
    s_loc = jnp.where(valid[:, :, None, :], s_loc + bias[None], NEG)
    s_ctx = jnp.einsum('brjqhd,blhd->bhrjql', qg, k_ctx, preferred_element_type=jnp.float32) * scale
    n_loc = kr * NA_KB
    logits = jnp.concatenate([s_loc.reshape(s_loc.shape[:5] + (n_loc,)), s_ctx], -1)
    p = jax.nn.softmax(logits, -1).astype(v.dtype)
    p_loc = p[..., :n_loc].reshape(s_loc.shape)
    p_ctx = p[..., n_loc:]
    o = (jnp.einsum('bhrjqkc,brkjchd->brjqhd', p_loc, v_blk)
         + jnp.einsum('bhrjql,blhd->brjqhd', p_ctx, v_ctx))
    return o.reshape(b, s, h * dh)

def _window_gqa(q, k, v, k_ctx, v_ctx, sink):
    b, s, hq, dh = q.shape
    hkv = k.shape[2]
    g = hq // hkv
    nb = s // GQA_BLOCK
    qb = q.reshape(b, nb, GQA_BLOCK, hkv, g, dh)

    def band(t):
        tp = jnp.pad(t, ((0, 0), (GQA_BLOCK, GQA_BLOCK), (0, 0), (0, 0)))
        tb = tp.reshape(b, nb + 2, GQA_BLOCK, hkv, dh)
        return jnp.concatenate([tb[:, :-2], tb[:, 1:-1], tb[:, 2:]], axis=2)

    kb, vb = band(k), band(v)
    q_pos = jnp.arange(s).reshape(nb, GQA_BLOCK)
    k_pos = (jnp.arange(nb)[:, None] - 1) * GQA_BLOCK + jnp.arange(3 * GQA_BLOCK)[None]
    kp = k_pos[:, None, :]
    valid = (jnp.abs(q_pos[:, :, None] - kp) <= GQA_WINDOW) & (kp >= 0) & (kp < s)
    scale = dh ** -0.5
    s_loc = jnp.einsum('bnqhgd,bnkhd->bnhgqk', qb, kb, preferred_element_type=jnp.float32) * scale
    s_loc = jnp.where(valid[None, :, None, None], s_loc, NEG)
    s_ctx = jnp.einsum('bnqhgd,blhd->bnhgql', qb, k_ctx, preferred_element_type=jnp.float32) * scale
    sk = jnp.broadcast_to(sink.reshape(hkv, g)[None, None, :, :, None, None].astype(jnp.float32),
                          s_loc.shape[:-1] + (1,))
    n_loc = 3 * GQA_BLOCK
    n_ctx = k_ctx.shape[1]
    p = jax.nn.softmax(jnp.concatenate([s_loc, s_ctx, sk], -1), -1).astype(v.dtype)
    o = (jnp.einsum('bnhgqk,bnkhd->bnqhgd', p[..., :n_loc], vb)
         + jnp.einsum('bnhgql,blhd->bnqhgd', p[..., n_loc:n_loc + n_ctx], v_ctx))
    return o.reshape(b, s, hq * dh)

def _even_mixer(h_lat, h_ctx, w_in, w_out, rpb, ctx_out):
    split_at = [FNET_WIDTH, FNET_WIDTH + NA_WIDTH, FNET_WIDTH + 2 * NA_WIDTH]
    f_l, q_l, k_l, v_l = jnp.split(h_lat @ w_in, split_at, -1)
    if ctx_out:
        f_c, q_c, k_c, v_c = jnp.split(h_ctx @ w_in, split_at, -1)
    else:
        k_c, v_c = jnp.split(h_ctx @ w_in[:, FNET_WIDTH + NA_WIDTH:], [NA_WIDTH], -1)
    k_c, v_c = _heads(k_c, NA_HEADS), _heads(v_c, NA_HEADS)
    na_l = _neighbourhood_attention(_heads(q_l, NA_HEADS), _heads(k_l, NA_HEADS), _heads(v_l, NA_HEADS), k_c, v_c, rpb)
    y_lat = jnp.concatenate([_fourier_mix(f_l), na_l], -1) @ w_out
    y_ctx = None
    if ctx_out:
        na_c = _ctx_attention(_heads(q_c, NA_HEADS), k_c, v_c)
        y_ctx = jnp.concatenate([_fourier_mix(f_c), na_c], -1) @ w_out
    return y_lat, y_ctx

def _odd_mixer(h_lat, h_ctx, w_in, w_out, sink, cos, sin, ctx_out):
    qw = GQA_Q_HEADS * HEAD_DIM
    kvw = GQA_KV_HEADS * HEAD_DIM
    q_l, k_l, v_l = jnp.split(h_lat @ w_in, [qw, qw + kvw], -1)
    q_l = _apply_rope(_heads(q_l, GQA_Q_HEADS), cos, sin)
    k_l = _apply_rope(_heads(k_l, GQA_KV_HEADS), cos, sin)
    if ctx_out:
        q_c, k_c, v_c = jnp.split(h_ctx @ w_in, [qw, qw + kvw], -1)
    else:
        k_c, v_c = jnp.split(h_ctx @ w_in[:, qw:], [kvw], -1)
    k_c, v_c = _heads(k_c, GQA_KV_HEADS), _heads(v_c, GQA_KV_HEADS)
    y_lat = _window_gqa(q_l, k_l, _heads(v_l, GQA_KV_HEADS), k_c, v_c, sink) @ w_out
    y_ctx = None
    if ctx_out:
        y_ctx = _ctx_attention(_heads(q_c, GQA_Q_HEADS), k_c, v_c, sink) @ w_out
    return y_lat, y_ctx

def _peer(h, w_q, sub_keys, u_tab, v_tab):
    b, l, d = h.shape
    q = (h @ w_q).reshape(b, l, PEER_HEADS, 2, PEER_QDIM // 2)
    s_half = jnp.einsum('blhpd,hpnd->blhpn', q, sub_keys, preferred_element_type=jnp.float32)
    top_s, top_i = lax.top_k(s_half, PEER_TOPK)
    cand_s = (top_s[..., 0, :, None] + top_s[..., 1, None, :]).reshape(b, l, PEER_HEADS, PEER_TOPK * PEER_TOPK)
    cand_i = (top_i[..., 0, :, None] * PEER_NKEYS + top_i[..., 1, None, :]).reshape(b, l, PEER_HEADS, PEER_TOPK * PEER_TOPK)
    best_s, best_pos = lax.top_k(cand_s, PEER_TOPK)
    expert = jnp.take_along_axis(cand_i, best_pos, -1)
    gate = jax.nn.softmax(best_s, -1).astype(h.dtype)
    n_chunks = (b * l) // PEER_TOKEN_CHUNK
    hk = PEER_HEADS * PEER_TOPK
    hc = h.reshape(n_chunks, PEER_TOKEN_CHUNK, d)
    ec = expert.reshape(n_chunks, PEER_TOKEN_CHUNK, hk)
    gc = gate.reshape(n_chunks, PEER_TOKEN_CHUNK, hk)

    def chunk(args):
        hx, ex, gx = args
        a = jnp.einsum('tkd,td->tk', u_tab[ex], hx)
        w = gx * jax.nn.gelu(a, approximate=False)
        return jnp.einsum('tk,tkd->td', w, v_tab[ex])

    return lax.map(chunk, (hc, ec, gc)).reshape(b, l, d)

def setup_inputs(seed: int = 0) -> dict:
    key = jax.random.key(seed)
    ks = jax.random.split(key, 22)
    d = D_MODEL

    def nrm(k, shape, scale):
        return jax.random.normal(k, shape, jnp.float32) * scale

    even_in = FNET_WIDTH + 3 * NA_WIDTH
    even_mix = FNET_WIDTH + NA_WIDTH
    odd_in = (GQA_Q_HEADS + 2 * GQA_KV_HEADS) * HEAD_DIM
    odd_mix = GQA_Q_HEADS * HEAD_DIM
    return {
        "x": nrm(ks[0], (BATCH, SEQ, d), 1.0),
        "c": nrm(ks[1], (BATCH, d), 1.0),
        "ctx": nrm(ks[2], (BATCH, CTX_LEN, d), 1.0),
        "c_ctx": nrm(ks[3], (d,), 1.0),
        "ada_w": nrm(ks[4], (DEPTH, d, 6 * d), d ** -0.5),
        "ada_b": nrm(ks[5], (DEPTH, 6 * d), 0.01),
        "post_ln_g": 1.0 + nrm(ks[6], (DEPTH, 2, d), 0.02),
        "post_ln_b": nrm(ks[7], (DEPTH, 2, d), 0.02),
        "even_w_in": nrm(ks[8], (N_EVEN, d, even_in), d ** -0.5),
        "even_w_out": nrm(ks[9], (N_EVEN, even_mix, d), DN_BETA * even_mix ** -0.5),
        "na_rpb": nrm(ks[10], (N_EVEN, NA_HEADS, 2 * NA_KR_MAX - 1, 2 * NA_KC - 1), 0.1),
        "odd_w_in": nrm(ks[11], (N_ODD, d, odd_in), d ** -0.5),
        "odd_w_out": nrm(ks[12], (N_ODD, odd_mix, d), DN_BETA * odd_mix ** -0.5),
        "gqa_sink": nrm(ks[13], (N_ODD, GQA_Q_HEADS), 1.0),
        "peer_w_q": nrm(ks[14], (DEPTH, d, PEER_HEADS * PEER_QDIM), d ** -0.5),
        "peer_sub_keys": nrm(ks[15], (DEPTH, PEER_HEADS, 2, PEER_NKEYS, PEER_QDIM // 2), (PEER_QDIM // 2) ** -0.5),
        "peer_u": nrm(ks[16], (DEPTH, PEER_EXPERTS, d), d ** -0.5),
        "peer_v": nrm(ks[17], (DEPTH, PEER_EXPERTS, d), DN_BETA),
    }

def reference(x, c, ctx, c_ctx, ada_w, ada_b, post_ln_g, post_ln_b, even_w_in, even_w_out, na_rpb,
              odd_w_in, odd_w_out, gqa_sink, peer_w_q, peer_sub_keys, peer_u, peer_v):
    cos, sin = _axial_rope_tables(x.shape[1])
    silu_c = jax.nn.silu(c)
    silu_cc = jax.nn.silu(c_ctx)
    h_ctx = ctx
    for layer in range(DEPTH):
        ctx_out = layer < DEPTH - 1
        i = layer // 2
        m_l = jnp.split((silu_c @ ada_w[layer] + ada_b[layer])[:, None, :], 6, -1)
        m_c = jnp.split((silu_cc @ ada_w[layer] + ada_b[layer])[None, None, :], 6, -1)
        a_l = _modulate(x, m_l[0], m_l[1])
        a_c = _modulate(h_ctx, m_c[0], m_c[1])
        if layer % 2 == 0:
            y_l, y_c = _even_mixer(a_l, a_c, even_w_in[i], even_w_out[i], na_rpb[i], ctx_out)
        else:
            y_l, y_c = _odd_mixer(a_l, a_c, odd_w_in[i], odd_w_out[i], gqa_sink[i], cos, sin, ctx_out)
        x = _layer_norm(DN_ALPHA * x + m_l[2] * y_l, post_ln_g[layer, 0], post_ln_b[layer, 0])
        f_l = _peer(_modulate(x, m_l[3], m_l[4]), peer_w_q[layer], peer_sub_keys[layer], peer_u[layer], peer_v[layer])
        x = _layer_norm(DN_ALPHA * x + m_l[5] * f_l, post_ln_g[layer, 1], post_ln_b[layer, 1])
        if ctx_out:
            h_ctx = _layer_norm(DN_ALPHA * h_ctx + m_c[2] * y_c, post_ln_g[layer, 0], post_ln_b[layer, 0])
            f_c = _peer(_modulate(h_ctx, m_c[3], m_c[4]), peer_w_q[layer], peer_sub_keys[layer], peer_u[layer], peer_v[layer])
            h_ctx = _layer_norm(DN_ALPHA * h_ctx + m_c[5] * f_c, post_ln_g[layer, 1], post_ln_b[layer, 1])
    return x


_drawn_inputs = setup_inputs


def setup_inputs(seed=0):
    import zlib

    import numpy as np

    out = dict(_drawn_inputs(seed))
    spreads = {}
    factors = {'na_rpb': 4.683, 'gqa_sink': 8.0}
    for name, (base, spread) in spreads.items():
        noise = np.random.default_rng([zlib.crc32(name.encode()), seed]).standard_normal(out[name].shape)
        drawn = base * np.exp(spread * noise) if base else spread * noise
        out[name] = __import__('jax').numpy.asarray(drawn.astype(out[name].dtype))
    for name, factor in factors.items():
        out[name] = (out[name] * factor).astype(out[name].dtype)
    return out
```

```python
import math
from contextlib import ExitStack

import numpy as np
import concourse.bass as bass
from concourse import mybir

F32 = mybir.dt.float32
U32 = mybir.dt.uint32
ALU = mybir.AluOpType
ACT = mybir.ActivationFunctionType
AX = mybir.AxisListType

P = 128
D = 1024
KB = D // P
SEQ, CTX = 512, 256
DEPTH = 2
GRID_W = 64
DH = 64
NA_HEADS, NA_KC, NA_KR = 8, 16, 8
FW = 512
QH, KVH = 16, 4
WINDOW = 128
PH, NKEYS, TOPK = 8, 128, 16
HK = PH * TOPK
EXPERTS = NKEYS * NKEYS
ALPHA = (2 * DEPTH) ** 0.25
EPS = 1e-6
NEG = -1e30
LOWEST = -3.0e38
CT, LT = CTX // P, SEQ // P
TILES = {"ctx": list(range(CT)), "lat": list(range(CT, CT + LT))}
ROW = {"lat": 0, "ctx": 1}
SHIFT1, SCALE1, GATE1, SHIFT2, SCALE2, GATE2 = range(6)
RPW = 2 * GRID_W - 1

WCH = KB * 512
WSLOT = WCH + 512
WRING = 3
URING, VRING, DRING = 8, 4, 4


def constants():
    t = {}
    t["ident"] = np.eye(P, dtype=np.float32)
    a = 2 * np.pi * np.outer(np.arange(DH), np.arange(DH)) / DH
    fc = np.zeros((P, 2, P))
    for g in range(2):
        s = slice(g * DH, (g + 1) * DH)
        fc[s, 0, s], fc[s, 1, s] = np.cos(a), np.sin(a)
    t["chan_dft"] = fc.reshape(P, 2 * P).astype(np.float32)
    for name, n in (("lat", SEQ), ("ctx", CTX)):
        k = (np.outer(np.arange(n), np.arange(n)) % n) * 2 * np.pi / n
        s = 1 / math.sqrt(n * DH)
        cs = np.stack([np.cos(k) * s, -np.sin(k) * s]).reshape(2, n // P, P, n)
        t["tok_dft_" + name] = cs.transpose(2, 0, 1, 3).reshape(P, -1).astype(np.float32)
    col = np.arange(GRID_W)
    start = np.clip(col - NA_KC // 2, 0, GRID_W - NA_KC)
    ok = (col[None] >= start[:, None]) & (col[None] < start[:, None] + NA_KC)
    t["col_mask"] = np.tile(np.where(ok, 0, NEG), (2, 1)).astype(np.float32)
    q, k = np.arange(P)[:, None], np.arange(P)[None]
    band = np.zeros((P, 3, P))
    band[:, 0][k < q], band[:, 2][k > q] = NEG, NEG
    t["band_mask"] = band.reshape(P, 3 * P).astype(np.float32)
    rot = np.zeros((P, P))
    for m in range(P):
        if m % DH < DH // 2:
            rot[m + DH // 2, m] = -1
        else:
            rot[m - DH // 2, m] = 1
    t["rotate_half"] = rot.astype(np.float32)
    n_freq = DH // 4
    inv = (np.float32(10000.0) ** (-np.arange(n_freq, dtype=np.float32) / np.float32(n_freq))).astype(np.float32)
    tok = np.arange(SEQ)
    ang = np.concatenate([(tok // GRID_W).astype(np.float32)[:, None] * inv,
                          (tok % GRID_W).astype(np.float32)[:, None] * inv], -1)
    rope = np.stack([np.cos(ang), np.sin(ang)]).astype(np.float32)
    t["rope"] = np.tile(rope.transpose(2, 0, 1), (4, 1, 1)).reshape(P, 2 * SEQ).copy()
    t["iota16"] = np.tile(np.arange(TOPK, dtype=np.float32), (P, 1))
    return t


def build(nc, I, out, mod_dram):
    es = ExitStack()
    with es:
        def sb(name, cols, dt=F32, rows=P):
            return es.enter_context(nc.sbuf_tensor(name, [rows, cols], dt))

        def sem(name):
            return es.enter_context(nc.semaphore(name))

        x_state = sb("x_state", (CT + LT) * D)
        wring = sb("wring", WRING * WSLOT)
        mixer = sb("mixer", 16384)
        ring = sb("ring", (URING + VRING) * D)
        ident = sb("ident", P)
        chan_dft = sb("chan_dft", 2 * P)
        col_mask = sb("col_mask", GRID_W)
        band_mask = sb("band_mask", 3 * P)
        rot = sb("rot", P)
        iota16 = sb("iota16", TOPK)
        sinks = sb("sinks", QH)
        sinks_exp = sb("sinks_exp", QH)
        silu_c = sb("silu_c", KB * 2)
        cc = sb("cc", KB * 2)
        cc_exp = sb("cc_exp", KB * 2)
        bnst = sb("bnst", LT * 12)
        mv = sb("mv", LT * 2)
        ve = sb("ve", LT)
        sd = sb("sd", LT)
        rs = sb("rs", LT)
        rt = sb("rt", LT)
        negm = sb("negm", QH * LT)
        den = sb("den", QH * LT)
        rden = sb("rden", QH * LT)
        acts = [sb(f"acts{i}", HK) for i in range(2)]
        gates = [sb(f"gates{i}", HK) for i in range(2)]
        idx_tok = [sb(f"idx_tok{i}", HK, U32) for i in range(2)]
        idx_f = sb("idx_f", HK)
        wts = [sb(f"wts{i}", HK) for i in range(2)]
        diags = sb("diags", DRING * P).rearrange("p (r n) -> p r n", r=DRING)
        stage_u = sb("stage_u", 2 * URING, U32)
        stage_v = sb("stage_v", 2 * URING, U32)
        tv = sb("tv", 2 * TOPK)
        tiu = sb("tiu", 2 * TOPK, U32)
        tif = sb("tif", 2 * TOPK)
        bv = sb("bv", HK)
        bpu = sb("bpu", TOPK, U32)
        bij_u = sb("bij_u", 2 * TOPK, U32)
        bij = sb("bij", 2 * TOPK)
        e12 = sb("e12", 2 * TOPK)
        gsum = sb("gsum", PH)

        def X(t):
            return x_state[:, t * D:(t + 1) * D]

        def Mx(a, n):
            return mixer[:, a:a + n]

        def view(ap, k):
            return ap.rearrange("p (k n) -> p k n", k=k)

        AT = view(Mx(0, 4096), 8)
        YT = view(Mx(4096, 4096), 8)
        FT_ = view(Mx(6144, 2048), 4)
        QT = view(Mx(8192, 2048), 4)
        KT = view(Mx(10240, 2048), 4)
        CKT = view(Mx(12288, 1024), 4)
        CV = view(Mx(13312, 1024), 2)
        VL = view(Mx(14336, 2048), 4)
        PQ = view(Mx(8192, 4096), 4)
        OTOK = view(Mx(0, 2048), 4)
        QT1 = view(Mx(4096, 4096), 8)
        KT1 = view(Mx(8192, 2048), 4)
        V1 = view(Mx(10240, 1024), 4)
        CKT1 = view(Mx(11264, 1024), 4)
        CV1 = view(Mx(12288, 512), 2)
        YT1 = view(Mx(4096, 4096), 8)
        OTOK1 = view(Mx(0, 4096), 4)
        H = view(Mx(4096, 4096), 4)
        SC = view(Mx(8192, 8192), 4)
        CAND = Mx(0, 256)
        OH = Mx(256, 256)
        S2 = Mx(512, 256)
        TMP = Mx(2048, 1024)
        HT = view(ring[:, 0:2048], 2)
        PR = view(ring[:, 2048:3584], 2)
        PT = view(ring[:, 3584:5120], 2)
        TB = view(ring[:, 5120:7168], 2)
        ROPE = view(ring[:, 7168:8192], 2)
        RA = ring[:, 8192:8704]
        RB = ring[:, 8704:9216]
        RTMP = ring[:, 9216:9728]
        PQT = view(ring[:, 8192:12288], 2)
        MODROW = mixer[0:2, 0:6 * D]
        ADAB = mixer[0:2, 6 * D:12 * D]
        UR = view(ring[:, 0:URING * D], URING)
        VR = view(ring[:, URING * D:(URING + VRING) * D], VRING)

        pairs = [es.enter_context(nc.psum_tensor(f"pair{i}", [P, 1024], F32)) for i in range(3)]
        facc = es.enter_context(nc.psum_tensor("facc", [P, 1024], F32))

        const_in, state_in, c_in = sem("const_in"), sem("state_in"), sem("c_in")
        adab_in, mod_out, modrow_free = sem("adab_in"), sem("mod_out"), sem("modrow_free")
        modrow_ready = sem("modrow_ready")
        cc_exp_done, silu_done = sem("cc_exp_done"), sem("silu_done")
        chunk_in = [sem(f"chunk_in{i}") for i in range(WRING)]
        vec_free = sem("vec_free")
        pair_full = [sem(f"pair_full{i}") for i in range(3)]
        pair_free = [sem(f"pair_free{i}") for i in range(3)]
        dve_step = sem("dve_step")
        ln_var, ln_sd = sem("ln_var"), sem("ln_sd")
        h_ready = sem("h_ready")
        at_ready = sem("at_ready")
        ev_ready = sem("ev_ready")
        rope_a, rope_b, rope_in = sem("rope_a"), sem("rope_b"), sem("rope_in")
        tb_in, tb_free = [sem(f"tb_in{i}") for i in range(2)], sem("tb_free")
        negm_ready, exp_done, pt_ready, pv_done = sem("negm_ready"), sem("exp_done"), sem("pt_ready"), sem("pv_done")
        sink_sub, sink_exp = sem("sink_sub"), sem("sink_exp")
        o_ready = sem("o_ready")
        x_done = sem("x_done")
        gate_sub, gate_exp = sem("gate_sub"), sem("gate_exp")
        idx_ready = sem("idx_ready")
        u_in = [sem(f"u_in{i}") for i in range(URING)]
        v_in = [sem(f"v_in{i}") for i in range(VRING)]
        u_used, v_used = sem("u_used"), sem("v_used")
        staged = sem("staged")
        acts_ready, gelu_done, wts_ready = sem("acts_ready"), sem("gelu_done"), sem("wts_ready")
        diag_ready, f_free = sem("diag_ready"), sem("f_free")
        out_done = sem("out_done")

        taken = {}

        def take(name, eng, s, n=1):
            taken[name, s.name] = taken.get((name, s.name), 0) + n
            eng.wait_ge(s, taken[name, s.name])

        chunks, chunk_no, chunk_freed, vecs_freed = [], {}, {}, [0]

        def chunk(name, *srcs):
            chunk_no[name] = len(chunks)
            chunks.append(srcs)

        def modvec(layer, stream, j):
            return bass.AP(mod_dram.tensor, ((layer * 2 + ROW[stream]) * 6 + j) * D, [[0, P], [1, D]])

        def postvec(which, layer, j):
            return bass.AP(I[which].tensor, (layer * 2 + j) * D, [[0, P], [1, D]])

        for layer in range(DEPTH):
            for n in range(12):
                chunk(("ada", layer, n), I["ada_w"][layer, n])
        for layer in range(DEPTH):
            for s in ("ctx", "lat"):
                chunk(("mod1", layer, s), modvec(layer, s, SHIFT1), modvec(layer, s, SCALE1))
                if layer == 0:
                    chunk(("w_in", 0, s, 0), I["even_w_in"][0])
                    chunk(("dft", s), I["tok_dft_" + s])
                    for n in range(1, 4):
                        chunk(("w_in", 0, s, n), I["even_w_in"][n])
                else:
                    for n in range(4) if s == "lat" else (2, 3):
                        chunk(("w_in", 1, s, n), I["odd_w_v"] if n == 3 else I["odd_w_in"][n])
                    if s == "ctx":
                        continue
                chunk(("res1", layer, s), modvec(layer, s, GATE1), postvec("post_g", layer, 0),
                      postvec("post_b", layer, 0))
                for n in range(2):
                    chunk(("w_out", layer, s, n), I["even_w_out" if layer == 0 else "odd_w_out"][n])
            for s in ("ctx", "lat") if layer == 0 else ("lat",):
                chunk(("mod2", layer, s), modvec(layer, s, SHIFT2), modvec(layer, s, SCALE2))
                for n in range(4):
                    chunk(("w_q", layer, s, n), I["peer_w_q"][layer, n])
                chunk(("res2", layer, s), modvec(layer, s, GATE2), postvec("post_g", layer, 1),
                      postvec("post_b", layer, 1))
        chunk_need, seen = [], [0] * WRING
        for n, srcs in enumerate(chunks):
            seen[n % WRING] += 16 * len(srcs)
            chunk_need.append(seen[n % WRING])

        def slot(eng, name):
            n = chunk_no[name]
            eng.wait_ge(chunk_in[n % WRING], chunk_need[n])
            return wring[:, (n % WRING) * WSLOT:(n % WRING + 1) * WSLOT]

        def vec(sl, j):
            return sl[:, j * D:(j + 1) * D]

        claimed, claims = {}, [0]

        def claim(pe, name):
            i, n = claims[0] % 3, claims[0] // 3
            claims[0] += 1
            claimed[name] = (i, n)
            if n:
                pe.wait_ge(pair_free[i], n)
            return pairs[i], pair_full[i]

        def filled(eng, name):
            i, n = claimed[name]
            eng.wait_ge(pair_full[i], n + 1)
            return pairs[i], pair_free[i], n + 1

        phases, tile_no = [], {}
        for layer in range(DEPTH):
            for s in ("ctx", "lat"):
                if layer == 1 and s == "ctx":
                    continue
                prev = None
                for t in TILES[s] + [None]:
                    if t is not None:
                        tile_no[layer, t] = len(tile_no)
                    phases.append((layer, s, t, prev))
                    prev = t
        u_groups, v_groups, nu, nv = {}, {}, 0, 0
        for ph in phases:
            u_groups[ph], v_groups[ph] = nu, nv
            nu += (HK // URING) * (ph[2] is not None)
            nv += (HK // VRING) * (ph[3] is not None)

        def stream_phases(layer, s):
            return [ph for ph in phases if ph[:2] == (layer, s)]

        block = es.enter_context(nc.Block())

        @block.tensor
        def _(pe):
            def mm(o, lhsT, rhs, start, stop):
                return nc.tensor.matmul(o, lhsT=lhsT, rhs=rhs, start=start, stop=stop, skip_group_check=True)

            def proj_features(name, dst_blocks, T, w, src):
                per = min(1024 // T, dst_blocks)
                for b0 in range(0, dst_blocks, per):
                    pair, full = claim(pe, name + (b0,))
                    for j in range(per):
                        for k in range(KB):
                            last = mm(pair[:, j * T:(j + 1) * T], w[:, k, (b0 + j) * P:(b0 + j + 1) * P],
                                      src[:, k, 0:T], k == 0, k == KB - 1)
                    last.then_inc(full, 1)
                return last

            def proj_tokens(name, nt, w, src, width, per):
                for t0 in range(0, nt, per):
                    pair, full = claim(pe, name + (t0,))
                    for j in range(per):
                        for k in range(KB):
                            last = mm(pair[:, j * 512:j * 512 + width], src[:, k, (t0 + j) * P:(t0 + j + 1) * P],
                                      w[:, k, :], k == 0, k == KB - 1)
                    last.then_inc(full, 1)
                return last

            def transpose_tiles(tag, layer, s):
                for i, t in enumerate(TILES[s]):
                    pair, full = claim(pe, (tag, layer, t))
                    take("pe", pe, h_ready)
                    src = HT[:, i % 2, :] if tag == "tr1" else H[:, i, :]
                    for k in range(KB):
                        last = nc.tensor.transpose(pair[:, k * P:(k + 1) * P], src[:, k * P:(k + 1) * P], ident[:])
                    last.then_inc(full, 1)
                take("pe", pe, at_ready, len(TILES[s]))

            def weights(name, cols=512):
                sl = slot(pe, name)
                return sl[:, 0:KB * cols].rearrange("p (k n) -> p k n", k=KB)

            def last_use(name):
                chunk_freed[name] = (claims[0] - 1) % 3, (claims[0] - 1) // 3 + 1

            def fourier(s, T):
                nt = T // P
                w = weights(("w_in", 0, s, 0))
                proj_features(("f", s), 4, T, w, AT)
                last_use(("w_in", 0, s, 0))
                take("pe", pe, ev_ready, max(1, 4 * T // 1024))
                for i in range(nt):
                    pair, full = claim(pe, ("chan", s, i))
                    for b in range(4):
                        last = mm(pair[:, b * 256:(b + 1) * 256], FT_[:, b, i * P:(i + 1) * P], chan_dft[:], True, True)
                    last.then_inc(full, 1)
                take("pe", pe, ev_ready, nt)
                sl = slot(pe, ("dft", s))
                w = sl[:, 0:2 * nt * T].rearrange("p (k n) -> p k n", k=2 * nt)
                per = 1024 // T
                for b0 in range(0, 4, per):
                    pair, full = claim(pe, ("tok", s, b0))
                    for j in range(per):
                        for k in range(2 * nt):
                            half, i = k // nt, k % nt
                            c = (b0 + j) * 256 + half * P
                            last = mm(pair[:, j * T:(j + 1) * T], PQ[:, i, c:c + P], w[:, k, :], k == 0, k == 2 * nt - 1)
                    last.then_inc(full, 1)
                last_use(("dft", s))
                take("pe", pe, ev_ready, max(1, 4 // per))

            def attention(units):
                def scores(u):
                    name, q, kl, lo, kc, _ = units[u]
                    pair, full = claim(pe, name + ("s",))
                    if kl is not None:
                        mm(pair[:, lo:512], q, kl, True, True)
                    mm(pair[:, 512:768], q, kc, True, True).then_inc(full, 1)

                scores(0)
                for u, (name, q, kl, lo, kc, vals) in enumerate(units):
                    if u + 1 < len(units):
                        scores(u + 1)
                    pair, full = claim(pe, name + ("t",))
                    take("pe", pe, exp_done)
                    for b in range(lo // P, 6):
                        last = nc.tensor.transpose(pair[:, b * P:(b + 1) * P], PR[:, u % 2, b * P:(b + 1) * P], ident[:])
                    last.then_inc(full, 1)
                    take("pe", pe, pt_ready)
                    for n, b in enumerate(range(lo // P, 6)):
                        last = mm(pair[:, 768:768 + DH], PT[:, u % 2, b * P:(b + 1) * P], vals[n], n == 0, b == 5)
                    last.then_inc(pv_done, 1)

            def out_transposes(tag, s, nb, otok):
                for i in range(len(TILES[s])):
                    take("pe", pe, o_ready)
                    pair, full = claim(pe, (tag, s, i))
                    for b in range(nb):
                        last = nc.tensor.transpose(pair[:, b * P:(b + 1) * P], otok[:, i, b * P:(b + 1) * P], ident[:])
                    last.then_inc(full, 1)
                take("pe", pe, ev_ready, len(TILES[s]))

            def w_out(layer, s, yt):
                for n in range(2):
                    w = weights(("w_out", layer, s, n))
                    proj_tokens(("y", layer, s, n), len(TILES[s]), w, yt, 512, 1)
                    last_use(("w_out", layer, s, n))

            def peer_front(layer, s):
                T = P * len(TILES[s])
                transpose_tiles("tr2", layer, s)
                for n in range(4):
                    sl = slot(pe, ("w_q", layer, s, n))
                    w = sl[:, 0:WCH].rearrange("p (k n) -> p k n", k=KB)
                    proj_features(("q", layer, s, n), 4, T, w, AT)
                    take("pe", pe, ev_ready, 4 * T // 1024)
                    pq = PQT[:, n % 2, :].rearrange("p (b t) -> p b t", b=4)
                    for i in range(len(TILES[s])):
                        pair, full = claim(pe, ("sc", layer, s, n, i))
                        for b in range(4):
                            last = mm(pair[:, b * P:(b + 1) * P], pq[:, b, i * P:(i + 1) * P],
                                      sl[:, WCH + b * P:WCH + (b + 1) * P], True, True)
                        last.then_inc(full, 1)
                    last_use(("w_q", layer, s, n))

            def peer_back(layer, s):
                for ph in stream_phases(layer, s):
                    _, _, t, prev = ph
                    if prev is None:
                        continue
                    n = tile_no[layer, prev]
                    if n:
                        pe.wait_ge(f_free, n)
                    base = 16 * v_groups[ph]

                    def accumulate(g, r, start):
                        pe.wait_ge(v_in[r % VRING], g * 32 + (16 * (r // VRING + 1) + base))
                        pe.wait_ge(diag_ready, g * 8 + (n * HK + r + 1))
                        for c in range(2):
                            last = mm(facc[:, c * 512:(c + 1) * 512], diags[:, r % DRING, :],
                                      VR[:, r % VRING, c * 512:(c + 1) * 512], start, False)
                        last.then_inc(v_used, 1)

                    for r in range(8):
                        accumulate(0, r, r == 0)
                    with pe.Fori(1, HK // 8) as g:
                        for r in range(8):
                            accumulate(g, r, False)

            pe.wait_ge(const_in, 16 * 8)
            take("pe", pe, silu_done)
            sc = silu_c[:].rearrange("p (k c) -> p k c", k=KB)
            for layer in range(DEPTH):
                for j in range(6):
                    pair, full = claim(pe, ("ada", layer, j))
                    for h in range(2):
                        w = weights(("ada", layer, 2 * j + h))
                        for k in range(KB):
                            last = mm(pair[0:2, h * 512:(h + 1) * 512], sc[:, k, :], w[:, k, :], k == 0, k == KB - 1)
                        last_use(("ada", layer, 2 * j + h))
                    last.then_inc(full, 1)

            for s in ("ctx", "lat"):
                T = P * len(TILES[s])
                nt = len(TILES[s])
                transpose_tiles("tr1", 0, s)
                fourier(s, T)
                for n in (1, 2):
                    proj_features(("qk", s, n), 4, T, weights(("w_in", 0, s, n)), AT)
                    last_use(("w_in", 0, s, n))
                proj_tokens(("v", s), nt, weights(("w_in", 0, s, 3)), AT, 512, 2)
                last_use(("w_in", 0, s, 3))
                take("pe", pe, ev_ready, 2 * (4 * T // 1024) + nt // 2)
                if s == "ctx":
                    units = [(("na", s, h, i), QT[64 * (h % 2):64 * (h % 2) + 64, h // 2, i * P:(i + 1) * P], None, 512,
                              CKT[64 * (h % 2):64 * (h % 2) + 64, h // 2, 0:CTX],
                              [CV[:, m, h * DH:(h + 1) * DH] for m in range(CT)])
                             for h in range(NA_HEADS) for i in range(nt)]
                else:
                    units = [(("na", s, h, i), QT[64 * (h % 2):64 * (h % 2) + 64, h // 2, i * P:(i + 1) * P],
                              KT[64 * (h % 2):64 * (h % 2) + 64, h // 2, :], 0,
                              CKT[64 * (h % 2):64 * (h % 2) + 64, h // 2, 0:CTX],
                              [VL[:, m, h * DH:(h + 1) * DH] for m in range(LT)]
                              + [CV[:, m, h * DH:(h + 1) * DH] for m in range(CT)])
                             for h in range(NA_HEADS) for i in range(nt)]
                attention(units)
                out_transposes("ot0", s, 4, OTOK)
                w_out(0, s, YT)
                if s == "lat":
                    pass
            for s in ("ctx", "lat"):
                peer_front(0, s)
                peer_back(0, s)

            transpose_tiles("tr1", 1, "ctx")
            proj_features(("ck", 1), 4, CTX, weights(("w_in", 1, "ctx", 2)), AT)
            last_use(("w_in", 1, "ctx", 2))
            proj_tokens(("cv", 1), CT, weights(("w_in", 1, "ctx", 3), 256), AT, 256, 2)
            last_use(("w_in", 1, "ctx", 3))
            take("pe", pe, ev_ready, 2)
            transpose_tiles("tr1", 1, "lat")
            for n in range(3):
                proj_features(("qk1", n), 4, SEQ, weights(("w_in", 1, "lat", n)), AT)
                last_use(("w_in", 1, "lat", n))
            proj_tokens(("v1",), LT, weights(("w_in", 1, "lat", 3), 256), AT, 256, 2)
            last_use(("w_in", 1, "lat", 3))
            take("pe", pe, ev_ready, 8)
            for b in range(12):
                pair, full = claim(pe, ("rope", b))
                src = QT1[:, b, :] if b < 8 else KT1[:, b - 8, :]
                mm(pair[:, 0:512], rot[:], src, True, True).then_inc(full, 1)
            take("pe", pe, rope_b, 12)
            units = []
            for i in range(LT):
                t0, t1 = max(i - 1, 0), min(i + 1, LT - 1)
                lo = 512 - (t1 - t0 + 1) * P
                for h in range(QH):
                    g, p0 = h // 4, 64 * (h % 2)
                    units.append((("gq", i, h), QT1[p0:p0 + 64, h // 2, i * P:(i + 1) * P],
                                  KT1[p0:p0 + 64, g, t0 * P:(t1 + 1) * P], lo, CKT1[p0:p0 + 64, g, 0:CTX],
                                  [V1[:, m, g * DH:(g + 1) * DH] for m in range(t0, t1 + 1)]
                                  + [CV1[:, m, g * DH:(g + 1) * DH] for m in range(CT)]))
            attention(units)
            out_transposes("ot1", "lat", 8, OTOK1)
            w_out(1, "lat", YT1)
            peer_front(1, "lat")
            peer_back(1, "lat")

        @block.scalar
        def _(act):
            def evac(name, dst, width=1024, scale=1.0, s=ev_ready, src=None):
                pair, free, n = filled(act, name)
                nc.scalar.activation(dst, (pair[:, 0:width] if src is None else src(pair)), ACT.Copy,
                                     scale=scale).then_inc(free, 1)
                act.wait_ge(free, n)
                nc.scalar.sem_inc(s, 1)

            def sqrt_of_variances(nt):
                take("act", act, ln_var)
                nc.scalar.activation(sd[:, 0:nt], ve[:, 0:nt], ACT.Sqrt).then_inc(ln_sd, 1)

            def evac_transposes(tag, layer, s):
                for i, t in enumerate(TILES[s]):
                    evac((tag, layer, t), AT[:, :, i * P:(i + 1) * P], s=at_ready,
                         src=lambda pair: pair[:].rearrange("p (k n) -> p k n", k=KB))

            def evac_blocks(name, dst, T, blocks=4, scale=1.0):
                per = min(1024 // T, blocks)
                for b0 in range(0, blocks, per):
                    evac(name + (b0,), dst[:, b0:b0 + per, 0:T], scale=scale,
                         src=lambda pair: pair[:, 0:per * T].rearrange("p (b t) -> p b t", b=per))

            def attention(units):
                def exps(u):
                    name, lo, j = units[u]
                    take("act", act, negm_ready)
                    i, n = claimed[name + ("s",)]
                    nc.scalar.activation(PR[:, u % 2, lo:768], pairs[i][:, lo:768], ACT.Exp,
                                         bias=negm[:, j:j + 1], accum_out=den[:, j:j + 1]).then_inc(pair_free[i], 1)
                    act.wait_ge(pair_free[i], n + 1)
                    nc.scalar.sem_inc(exp_done, 1)

                base = taken.get(("act", "pv_base"), 0)
                exps(0)
                for u, (name, lo, j) in enumerate(units):
                    if u + 1 < len(units):
                        exps(u + 1)
                    i, n = claimed[name + ("t",)]
                    act.wait_ge(pair_full[i], n + 1)
                    if u >= 2:
                        act.wait_ge(pv_done, base + u - 1)
                    nc.scalar.activation(PT[:, u % 2, lo:768], pairs[i][:, lo:768], ACT.Copy).then_inc(pt_ready, 1)
                taken[("act", "pv_base")] = base + len(units)

            def peer_front(layer, s):
                T = P * len(TILES[s])
                sqrt_of_variances(len(TILES[s]))
                evac_transposes("tr2", layer, s)
                for n in range(4):
                    evac_blocks(("q", layer, s, n), PQT[:, n % 2, :].rearrange("p (b t) -> p b t", b=4), T)
                    for i in range(len(TILES[s])):
                        evac(("sc", layer, s, n, i), SC[:, i, n * 512:(n + 1) * 512], 512, s=gate_sub)

            def peer_back(layer, s):
                tiles = TILES[s]

                def finish_topk(t):
                    take("act", act, gate_exp)
                    b = tile_no[layer, t] % 2
                    nc.scalar.activation(gates[b][:], gates[b][:], ACT.Exp).then_inc(gelu_done, 1)

                finish_topk(tiles[0])
                for ph in stream_phases(layer, s):
                    _, _, t, prev = ph
                    if prev is not None:
                        n = tile_no[layer, prev]
                        act.wait_ge(wts_ready, n + 1)
                        with act.Fori(0, HK // DRING) as g:
                            for r in range(DRING):
                                act.wait_ge(v_used, g * DRING + (n * HK + r + 1 + VRING - DRING))
                                nc.scalar.activation(diags[:, r, :], ident[:], ACT.Copy,
                                                     scale=wts[n % 2][:, bass.ds(g * DRING + r, 1)],
                                                     ).then_inc(diag_ready, 1)
                    if t is not None:
                        b = tile_no[layer, t] % 2
                        nxt = tiles.index(t) + 1
                        if nxt < len(tiles):
                            finish_topk(tiles[nxt])
                        take("act", act, acts_ready)
                        nc.scalar.activation(acts[b][:], acts[b][:], ACT.Gelu).then_inc(gelu_done, 1)
                    if prev is not None:
                        sqrt_of_variances(1)

            act.wait_ge(c_in, 16)
            nc.scalar.activation(cc_exp[:], cc[:], ACT.Exp, scale=-1.0).then_inc(cc_exp_done, 1)

            for s in ("ctx", "lat"):
                T, nt = P * len(TILES[s]), len(TILES[s])
                sqrt_of_variances(nt)
                evac_transposes("tr1", 0, s)
                evac_blocks(("f", s), FT_, T)
                for i in range(nt):
                    evac(("chan", s, i), PQ[:, i, :])
                per = 1024 // T
                for b0 in range(0, 4, per):
                    evac(("tok", s, b0), YT[:, b0:b0 + per, 0:T],
                         src=lambda pair: pair[:].rearrange("p (b t) -> p b t", b=per))
                evac_blocks(("qk", s, 1), QT, T, scale=DH ** -0.5)
                evac_blocks(("qk", s, 2), KT if s == "lat" else CKT, T)
                V = VL if s == "lat" else CV
                for i in range(0, nt, 2):
                    evac(("v", s, i), V[:, i:i + 2, :], src=lambda pair: pair[:].rearrange("p (t n) -> p t n", t=2))
                lo = 0 if s == "lat" else 512
                attention([(("na", s, h, i), lo, h * LT + i) for h in range(NA_HEADS) for i in range(nt)])
                for i in range(nt):
                    evac(("ot0", s, i), YT[:, 4:8, i * P:(i + 1) * P],
                         src=lambda pair: pair[:, 0:512].rearrange("p (b t) -> p b t", b=4))
                sqrt_of_variances(nt)
            for s in ("ctx", "lat"):
                peer_front(0, s)
                peer_back(0, s)

            sqrt_of_variances(CT)
            evac_transposes("tr1", 1, "ctx")
            evac_blocks(("ck", 1), CKT1, CTX)
            evac(("cv", 1, 0), CV1, src=lambda pair: pair[:].rearrange("p (t n) -> p t n", t=2)[:, :, 0:256])
            sqrt_of_variances(LT)
            evac_transposes("tr1", 1, "lat")
            for n in range(2):
                evac_blocks(("qk1", n), QT1[:, 4 * n:4 * n + 4, :], SEQ, scale=DH ** -0.5)
            evac_blocks(("qk1", 2), KT1, SEQ)
            for i in range(0, LT, 2):
                evac(("v1", i), V1[:, i:i + 2, :],
                     src=lambda pair: pair[:].rearrange("p (t n) -> p t n", t=2)[:, :, 0:256])
            units = []
            for i in range(LT):
                lo = 512 - (min(i + 1, LT - 1) - max(i - 1, 0) + 1) * P
                units += [(("gq", i, h), lo, i * QH + h) for h in range(QH)]
            attention(units)
            for i in range(LT):
                take("act", act, sink_sub)
                nc.scalar.activation(sinks_exp[:], sinks_exp[:], ACT.Exp).then_inc(sink_exp, 1)
            for i in range(LT):
                evac(("ot1", "lat", i), YT1[:, :, i * P:(i + 1) * P],
                     src=lambda pair: pair[:].rearrange("p (b t) -> p b t", b=8))
            sqrt_of_variances(LT)
            peer_front(1, "lat")
            peer_back(1, "lat")

        @block.vector
        def _(v):
            V = nc.vector
            done = [0]

            def step(ins):
                done[0] += 1
                ins.then_inc(dve_step, 1)
                v.wait_ge(dve_step, done[0])

            def signal(ins, s):
                step(ins)
                V.sem_inc(s, 1)

            def statistics(tiles):
                n = len(tiles)
                st = bnst[:].rearrange("p (t h s) -> p t h s", t=LT, h=2)
                m = mv[:].rearrange("p (t c) -> p t c", c=2)
                for i, t in enumerate(tiles):
                    for h in range(2):
                        step(V.bn_stats(st[:, i, h, :], X(t)[:, h * 512:(h + 1) * 512]))
                    step(V.bn_aggr(m[:, i, :], bnst[:, i * 12:(i + 1) * 12]))
                var = ve[:, 0:n].unsqueeze(2)
                signal(V.tensor_scalar(var, m[:, 0:n, 1:2], EPS, None, ALU.add), ln_var)
                take("dve", v, ln_sd)
                step(V.reciprocal(rs[:, 0:n], sd[:, 0:n]))
                step(V.tensor_tensor(rt[:, 0:n], rs[:, 0:n], rs[:, 0:n], ALU.mult))
                step(V.tensor_tensor(rt[:, 0:n], rt[:, 0:n], ve[:, 0:n], ALU.mult))
                step(V.tensor_scalar(rt[:, 0:n], rt[:, 0:n], -0.5, 1.5, ALU.mult, ALU.add))
                step(V.tensor_tensor(rs[:, 0:n], rs[:, 0:n], rt[:, 0:n], ALU.mult))

            def normalise(i, t, dst, scale, shift):
                step(V.tensor_scalar(dst, X(t), mv[:, 2 * i:2 * i + 1], rs[:, i:i + 1], ALU.subtract, ALU.mult))
                step(V.tensor_tensor(dst, dst, scale, ALU.mult))
                return V.tensor_tensor(dst, dst, shift, ALU.add)

            def free(name):
                vecs_freed[0] += 1
                chunk_freed[name] = vecs_freed[0]
                V.sem_inc(vec_free, 1)

            def modulate(tag, layer, s):
                statistics(TILES[s])
                name = ("mod1" if tag == "tr1" else "mod2", layer, s)
                sl = slot(v, name)
                for i, t in enumerate(TILES[s]):
                    if tag == "tr1" and i >= 2:
                        filled(v, (tag, layer, TILES[s][i - 2]))
                    dst = HT[:, i % 2, :] if tag == "tr1" else H[:, i, :]
                    signal(normalise(i, t, dst, vec(sl, 1), vec(sl, 0)), h_ready)
                free(name)

            def residual_out(layer, s):
                name = ("res1", layer, s)
                sl = slot(v, name)
                for n in range(2):
                    cols = slice(n * 512, (n + 1) * 512)
                    for i, t in enumerate(TILES[s]):
                        pair, fr, cnt = filled(v, ("y", layer, s, n, i))
                        V.tensor_tensor(RTMP, pair[:, 0:512], vec(sl, 0)[:, cols], ALU.mult).then_inc(fr, 1)
                        v.wait_ge(fr, cnt)
                        step(V.scalar_tensor_tensor(X(t)[:, cols], X(t)[:, cols], ALPHA, RTMP, ALU.mult, ALU.add))
                statistics(TILES[s])
                for i, t in enumerate(TILES[s]):
                    step(normalise(i, t, X(t), vec(sl, 1), vec(sl, 2)))
                free(name)

            def attention(units):
                def scores(u):
                    name, lo, hi, mask, j = units[u]
                    pair, fr, n = filled(v, name + ("s",))
                    if mask is not None:
                        m = mask() if callable(mask) else mask
                        step(V.tensor_tensor(pair[:, lo:hi], pair[:, lo:hi], m, ALU.add))
                    signal(V.tensor_reduce(negm[:, j:j + 1], pair[:, lo:768], AX.X, ALU.max, negate=True),
                           sink_exp if False else dve_neg)

                scores(0)
                for u in range(len(units)):
                    if u + 1 < len(units):
                        scores(u + 1)
                    yield u

            dve_neg = negm_ready

            def copy_out(name, dst):
                take("dve", v, pv_done)
                i, n = claimed[name + ("t",)]
                V.tensor_copy(dst, pairs[i][:, 768:768 + DH]).then_inc(pair_free[i], 1)
                v.wait_ge(pair_free[i], n + 1)

            def top16(vals, idxs, src, n):
                step(V.max(vals[:, 0:8], src))
                step(V.max_index(idxs[:, 0:8], vals[:, 0:8], src))
                step(V.match_replace(S2[:, 0:n], vals[:, 0:8], src, LOWEST))
                step(V.max(vals[:, 8:16], S2[:, 0:n]))
                step(V.max_index(idxs[:, 8:16], vals[:, 8:16], S2[:, 0:n]))

            def topk_head(i, h):
                for p in range(2):
                    src = SC[:, i, (2 * h + p) * P:(2 * h + p + 1) * P]
                    top16(tv[:, p * TOPK:(p + 1) * TOPK], tiu[:, p * TOPK:(p + 1) * TOPK], src, P)
                step(V.tensor_copy(tif[:], tiu[:]))
                wide = [P, TOPK, TOPK]
                cand = CAND.rearrange("p (i j) -> p i j", i=TOPK)
                oh = OH.rearrange("p (k i) -> p k i", k=TOPK)
                step(V.tensor_tensor(cand, tv[:, 0:TOPK].unsqueeze(2).to_broadcast(wide),
                                     tv[:, TOPK:].unsqueeze(1).to_broadcast(wide), ALU.add))
                best = bv[:, h * TOPK:(h + 1) * TOPK]
                top16(best, bpu[:], CAND, TOPK * TOPK)
                step(V.tensor_scalar(bij_u[:, 0:TOPK], bpu[:], 4, None, ALU.logical_shift_right))
                step(V.tensor_scalar(bij_u[:, TOPK:], bpu[:], 15, None, ALU.bitwise_and))
                step(V.tensor_copy(bij[:], bij_u[:]))
                for p in range(2):
                    sl = slice(p * TOPK, (p + 1) * TOPK)
                    step(V.tensor_tensor(oh, bij[:, sl].unsqueeze(2).to_broadcast(wide),
                                         iota16[:].unsqueeze(1).to_broadcast(wide), ALU.is_equal))
                    step(V.tensor_tensor(oh, oh, tif[:, sl].unsqueeze(1).to_broadcast(wide), ALU.mult))
                    step(V.tensor_reduce(e12[:, sl], oh, AX.X, ALU.add))
                step(V.scalar_tensor_tensor(idx_f[:, h * TOPK:(h + 1) * TOPK], e12[:, 0:TOPK], float(NKEYS),
                                            e12[:, TOPK:], ALU.mult, ALU.add))

            def topk_finish(layer, t):
                b = tile_no[layer, t] % 2
                wide = [P, PH, TOPK]
                hv = bv[:].rearrange("p (h k) -> p h k", h=PH)
                gv = gates[b][:].rearrange("p (h k) -> p h k", h=PH)
                step(V.tensor_copy(idx_tok[b][:], idx_f[:]))
                V.sem_inc(idx_ready, 1)
                step(V.tensor_tensor(gv, hv, hv[:, :, 0:1].to_broadcast(wide), ALU.subtract))
                V.sem_inc(gate_exp, 1)
                take("dve", v, gelu_done)
                step(V.tensor_reduce(gsum[:], gv, AX.X, ALU.add))
                step(V.reciprocal(gsum[:], gsum[:]))
                step(V.tensor_tensor(gv, gv, gsum[:].unsqueeze(2).to_broadcast(wide), ALU.mult))

            def peer_back(layer, s):
                tiles = TILES[s]
                take("dve", v, gate_sub, 4 * len(tiles))
                for h in range(PH):
                    topk_head(0, h)
                topk_finish(layer, tiles[0])
                name = ("res2", layer, s)
                sl = None
                for ph in stream_phases(layer, s):
                    _, _, t, prev = ph
                    if t is not None:
                        i, b = tiles.index(t), tile_no[layer, t] % 2
                        for seg in range(PH):
                            base = 16 * (u_groups[ph] + 2 * seg) + 16
                            with v.Fori(0, 2) as g:
                                for r in range(URING):
                                    v.wait_ge(u_in[r], g * 16 + base)
                                    V.scalar_tensor_tensor(
                                        UR[:, r, :], UR[:, r, :], 1.0, H[:, i, :], ALU.mult, ALU.mult,
                                        accum_out=acts[b][:, bass.ds(g * URING + (seg * 2 * URING + r), 1)],
                                    ).then_inc(u_used, 1)
                            if i + 1 < len(tiles):
                                topk_head(i + 1, seg)
                        v.wait_ge(u_used, URING + HK * (tile_no[layer, t] + 1))
                        if i + 1 < len(tiles):
                            topk_finish(layer, tiles[i + 1])
                        V.sem_inc(acts_ready, 1)
                        take("dve", v, gelu_done)
                        step(V.tensor_tensor(wts[b][:], acts[b][:], gates[b][:], ALU.mult))
                        V.sem_inc(wts_ready, 1)
                    if prev is not None:
                        sl = slot(v, name)
                        n = tile_no[layer, prev] + 1
                        v.wait_ge(v_used, VRING + HK * n)
                        V.tensor_tensor(TMP, facc[:], vec(sl, 0), ALU.mult).then_inc(f_free, 1)
                        v.wait_ge(f_free, n)
                        step(V.scalar_tensor_tensor(X(prev), X(prev), ALPHA, TMP, ALU.mult, ALU.add))
                        statistics([prev])
                        signal(normalise(0, prev, X(prev), vec(sl, 1), vec(sl, 2)), x_done)
                free(name)

            V.sem_inc(u_used, URING)
            v.wait_ge(const_in, 16 * 8)
            take("dve", v, cc_exp_done)
            step(V.tensor_scalar(silu_c[:], cc_exp[:], 1.0, None, ALU.add))
            step(V.reciprocal(silu_c[:], silu_c[:]))
            signal(V.tensor_tensor(silu_c[:], silu_c[:], cc[:], ALU.mult), silu_done)
            for layer in range(DEPTH):
                v.wait_ge(adab_in, 16 * (layer + 1))
                if layer:
                    v.wait_ge(mod_out, 16)
                for j in range(6):
                    pair, fr, n = filled(v, ("ada", layer, j))
                    one = 1.0 if j in (SCALE1, SCALE2) else 0.0
                    V.scalar_tensor_tensor(MODROW[:, j * D:(j + 1) * D], pair[0:2, :], one,
                                           ADAB[:, j * D:(j + 1) * D], ALU.add, ALU.add).then_inc(fr, 1)
                    v.wait_ge(fr, n)
                V.sem_inc(modrow_ready, 1)
            v.wait_ge(state_in, 32)
            v.wait_ge(mod_out, 32)

            for s in ("ctx", "lat"):
                nt = len(TILES[s])
                modulate("tr1", 0, s)
                units = []
                lo = 0 if s == "lat" else 512

                def head_bias(h):
                    def get():
                        return None
                    return get

                names = [("na", s, h, i) for h in range(NA_HEADS) for i in range(nt)]
                for h in range(NA_HEADS):
                    for i in range(nt):
                        m = None
                        if s == "lat":
                            j0 = (NA_KR - 1 - 2 * i) * GRID_W
                            m = TB[:, h % 2, j0:j0 + NA_KR * GRID_W]
                        units.append((("na", s, h, i), lo, 512, m, h * LT + i))
                if s == "lat":
                    def prep_bias(h):
                        v.wait_ge(tb_in[h % 2], 32 * (h // 2 + 1))
                        tb = TB[:, h % 2, :].rearrange("p (j c) -> p j c", c=GRID_W)
                        step(V.tensor_tensor(tb, tb, col_mask[:].unsqueeze(1).to_broadcast([P, 16, GRID_W]), ALU.add))

                    prep_bias(0)
                for u in attention(units):
                    name = units[u][0]
                    h, i = name[2], name[3]
                    if s == "lat" and i == LT - 2 and h + 1 < NA_HEADS:
                        prep_bias(h + 1)
                    copy_out(name, OTOK[:, i, h * DH:(h + 1) * DH])
                    if s == "lat" and i == LT - 1:
                        V.sem_inc(tb_free, 1)
                step(V.reciprocal(rden[:, 0:NA_HEADS * LT], den[:, 0:NA_HEADS * LT]) if s == "lat" else
                     V.reciprocal(rden[:, 0:NA_HEADS * LT].rearrange("p (h i) -> p h i", h=NA_HEADS)[:, :, 0:nt],
                                  den[:, 0:NA_HEADS * LT].rearrange("p (h i) -> p h i", h=NA_HEADS)[:, :, 0:nt]))
                for i in range(nt):
                    o = OTOK[:, i, :].rearrange("p (h d) -> p h d", h=NA_HEADS)
                    r = rden[:, 0:NA_HEADS * LT].rearrange("p (h i) -> p h i", h=NA_HEADS)[:, :, i:i + 1]
                    signal(V.tensor_tensor(o, o, r.to_broadcast([P, NA_HEADS, DH]), ALU.mult), o_ready)
                residual_out(0, s)
            for s in ("ctx", "lat"):
                modulate("tr2", 0, s)
                peer_back(0, s)

            modulate("tr1", 1, "ctx")
            modulate("tr1", 1, "lat")
            v.wait_ge(rope_in, 16)
            for b in range(12):
                src = QT1[:, b, :] if b < 8 else KT1[:, b - 8, :]
                pair, fr, n = filled(v, ("rope", b))
                V.tensor_tensor(RA, pair[:, 0:512], ROPE[:, 1, :], ALU.mult).then_inc(fr, 1)
                v.wait_ge(fr, n)
                step(V.tensor_tensor(RB, src, ROPE[:, 0, :], ALU.mult))
                signal(V.tensor_tensor(src, RA, RB, ALU.add), rope_b)
            units = []
            for i in range(LT):
                t0, t1 = max(i - 1, 0), min(i + 1, LT - 1)
                lo = 512 - (t1 - t0 + 1) * P
                m0 = (t0 - i + 1) * P
                units += [(("gq", i, h), lo, 512, band_mask[:, m0:m0 + 512 - lo], i * QH + h) for h in range(QH)]
            for u in sink_attention(V, v, units, step, signal, filled, negm, sinks, negm_ready, AX, ALU):
                name = units[u][0]
                copy_out(name, OTOK1[:, name[1], name[2] * DH:(name[2] + 1) * DH])
            for i in range(LT):
                r = slice(i * QH, (i + 1) * QH)
                signal(V.tensor_tensor(sinks_exp[:], sinks[:], negm[:, r], ALU.add), sink_sub)
                take("dve", v, sink_exp)
                step(V.tensor_tensor(den[:, r], den[:, r], sinks_exp[:], ALU.add))
                step(V.reciprocal(rden[:, r], den[:, r]))
                o = OTOK1[:, i, :].rearrange("p (h d) -> p h d", h=QH)
                signal(V.tensor_tensor(o, o, rden[:, r].unsqueeze(2).to_broadcast([P, QH, DH]), ALU.mult), o_ready)
            residual_out(1, "lat")
            modulate("tr2", 1, "lat")
            peer_back(1, "lat")

        @block.gpsimd
        def _(pool):
            need_u = es.enter_context(pool.register("need_u"))
            need_v = es.enter_context(pool.register("need_v"))
            need_staged = es.enter_context(pool.register("need_staged"))
            pool.sem_inc(v_used, VRING)
            pool.reg_mov(need_u, 1)
            pool.reg_mov(need_v, 1)
            staged_before = 0
            for ph in phases:
                layer, s, t, prev = ph
                if t is not None:
                    bu = tile_no[layer, t] % 2
                    pool.wait_ge(idx_ready, tile_no[layer, t] + 1)
                if prev is not None:
                    bw = tile_no[layer, prev] % 2
                both = (t is not None) + (prev is not None)
                pool.reg_mov(need_staged, staged_before + both)
                staged_before += both * HK // URING
                with pool.Fori(0, HK // (2 * URING)) as g:
                    for half in range(2):
                        cols = slice(half * URING, (half + 1) * URING)
                        src = bass.ds(g * 2 * URING + half * URING, URING)
                        if t is not None:
                            nc.gpsimd.tensor_copy(stage_u[:, cols], idx_tok[bu][:, src]).then_inc(staged, 1)
                        if prev is not None:
                            nc.gpsimd.tensor_copy(stage_v[:, cols], idx_tok[bw][:, src]).then_inc(staged, 1)
                        pool.wait_ge(staged, need_staged)
                        pool.reg_add(need_staged, need_staged, both)
                        for r in range(URING):
                            j = half * URING + r
                            if t is not None:
                                pool.wait_ge(u_used, need_u)
                                pool.reg_add(need_u, need_u, 1)
                                pool.indirect_dma_start(
                                    UR[:, r, :], None, I[f"peer_u{layer}"],
                                    bass.IndirectOffsetOnAxis(ap=stage_u[:, j:j + 1], axis=0)).then_inc(u_in[r], 16)
                            if prev is not None:
                                pool.wait_ge(v_used, need_v)
                                pool.reg_add(need_v, need_v, 1)
                                pool.indirect_dma_start(
                                    VR[:, r % VRING, :], None, I[f"peer_v{layer}"],
                                    bass.IndirectOffsetOnAxis(ap=stage_v[:, j:j + 1], axis=0),
                                ).then_inc(v_in[r % VRING], 16)

        @block.sync
        def _(sp):
            sp.dma_start(cc[:], I["cc"]).then_inc(c_in, 16)
            for dst, name in ((ident, "ident"), (chan_dft, "chan_dft"), (col_mask, "col_mask"),
                              (band_mask, "band_mask"), (rot, "rotate_half"), (iota16, "iota16")):
                sp.dma_start(dst[:], I[name]).then_inc(const_in, 16)
            sp.dma_start(sinks[:], bass.AP(I["gqa_sink"].tensor, 0, [[0, P], [1, QH]])).then_inc(const_in, 16)
            sp.dma_start(sinks_exp[:], bass.AP(I["gqa_sink"].tensor, 0, [[0, P], [1, QH]])).then_inc(const_in, 16)

            names = list(chunk_no)

            def load(n):
                if n >= WRING:
                    freed = chunk_freed[names[n - WRING]]
                    if isinstance(freed, tuple):
                        sp.wait_ge(pair_full[freed[0]], freed[1])
                    else:
                        sp.wait_ge(vec_free, freed)
                for j, src in enumerate(chunks[n]):
                    w = src.shape[-1]
                    a = (n % WRING) * WSLOT + j * D
                    sp.dma_start(wring[:, a:a + w], src).then_inc(chunk_in[n % WRING], 16)

            def adab(layer):
                src = bass.AP(I["ada_b"].tensor, layer * 6 * D, [[0, 2], [1, 6 * D]])
                sp.dma_start(ADAB, src).then_inc(adab_in, 16)

            def store_rows(layer):
                sp.wait_ge(modrow_ready, layer + 1)
                dst = bass.AP(mod_dram.tensor, layer * 12 * D, [[6 * D, 2], [1, 6 * D]])
                sp.dma_start(dst, MODROW).then_inc(mod_out, 16)

            adab(0)
            for n in range(3):
                load(n)
            sp.dma_start(x_state[:, 0:CT * D].rearrange("p (t d) -> p t d", t=CT),
                         I["ctx"].rearrange("(t p) d -> p t d", p=P)).then_inc(state_in, 16)
            sp.dma_start(x_state[:, CT * D:].rearrange("p (t d) -> p t d", t=LT),
                         I["x"].rearrange("(t p) d -> p t d", p=P)).then_inc(state_in, 16)
            for n in range(3, 12):
                load(n)
            store_rows(0)
            adab(1)
            for n in range(12, 24):
                load(n)
            store_rows(1)
            sp.wait_ge(mod_out, 32)
            for n in range(24, len(chunks)):
                name = names[n]
                if name == ("res1", 0, "lat"):
                    for h in range(NA_HEADS):
                        if h >= 2:
                            sp.wait_ge(tb_free, h - 1)
                        for a in range(2):
                            src = I["rpb"][h][:, (1 - a) * GRID_W:(17 - a) * GRID_W]
                            sp.dma_start(TB[64 * a:64 * a + 64, h % 2, :], src).then_inc(tb_in[h % 2], 16)
                if name == ("res1", 1, "lat"):
                    sp.wait_ge(x_done, CT + LT)
                    sp.dma_start(ring[:, 7168:8192], I["rope"]).then_inc(rope_in, 16)
                load(n)
            for i in range(LT):
                sp.wait_ge(x_done, CT + LT + i + 1)
                sp.dma_start(out[i * P:(i + 1) * P, :], X(CT + i)).then_inc(out_done, 16)
            sp.wait_ge(out_done, 16 * LT)


def sink_attention(V, v, units, step, signal, filled, negm, sinks, negm_ready, AX, ALU):
    def scores(u):
        name, lo, hi, mask, j = units[u]
        pair, fr, n = filled(v, name + ("s",))
        h = name[2]
        step(V.tensor_tensor(pair[:, lo:hi], pair[:, lo:hi], mask, ALU.add))
        step(V.tensor_reduce(negm[:, j:j + 1], pair[:, lo:768], AX.X, ALU.max, negate=False))
        signal(V.tensor_scalar(negm[:, j:j + 1], negm[:, j:j + 1], sinks[:, h:h + 1], -1.0, ALU.max, ALU.mult),
               negm_ready)

    scores(0)
    for u in range(len(units)):
        if u + 1 < len(units):
            scores(u + 1)
        yield u


def chunked(w, cols=512):
    n = w.shape[1] // cols
    return np.ascontiguousarray(w.reshape(KB, P, n, cols).transpose(2, 1, 0, 3).reshape(n, P, KB * cols))


def layout(inputs):
    a = {k: np.asarray(v) for k, v in inputs.items()}
    t = constants()
    t["x"] = a["x"][0]
    t["ctx"] = a["ctx"][0]
    t["cc"] = np.stack([a["c"][0].reshape(KB, P), a["c_ctx"].reshape(KB, P)], -1).transpose(1, 0, 2).reshape(P, KB * 2)
    t["ada_w"] = np.stack([chunked(a["ada_w"][l]) for l in range(DEPTH)])
    t["ada_b"] = a["ada_b"]
    t["post_g"], t["post_b"] = a["post_ln_g"], a["post_ln_b"]
    t["even_w_in"], t["even_w_out"] = chunked(a["even_w_in"][0]), chunked(a["even_w_out"][0])
    w = a["odd_w_in"][0]
    kw = w[:, QH * DH:(QH + KVH) * DH].reshape(D, KVH, 1, DH)
    kw = np.concatenate([kw, kw], 2).reshape(D, 512)
    t["odd_w_in"] = np.concatenate([chunked(w[:, :QH * DH]), chunked(kw)])
    t["odd_w_v"] = chunked(w[:, (QH + KVH) * DH:], 256)[0]
    t["odd_w_out"] = chunked(a["odd_w_out"][0])
    t["gqa_sink"] = a["gqa_sink"]
    rpb = a["na_rpb"][0]
    pad = np.zeros((NA_HEADS, 17, RPW), np.float32)
    c0 = GRID_W - NA_KC
    pad[:, 1:16, c0:c0 + 2 * NA_KC - 1] = rpb
    t["rpb"] = np.stack([pad[:, :, GRID_W - 1 - c:RPW - c] for c in range(GRID_W)], 1).reshape(NA_HEADS, GRID_W, -1)
    wq = np.stack([chunked(a["peer_w_q"][l]) for l in range(DEPTH)])
    sk = a["peer_sub_keys"].transpose(0, 4, 1, 2, 3).reshape(DEPTH, P, 4, 512).transpose(0, 2, 1, 3)
    t["peer_w_q"] = np.concatenate([wq, sk], -1)
    for l in range(DEPTH):
        t[f"peer_u{l}"], t[f"peer_v{l}"] = a["peer_u"][l], a["peer_v"][l]
    return {k: np.ascontiguousarray(v) for k, v in t.items()}


def kernel(**inputs):
    import concourse.bacc as bacc
    from concourse.bass_utils import run_bass_kernel_spmd

    nc = bacc.Bacc("TRN2", target_bir_lowering=False, num_devices=1)
    arrays = layout(inputs)
    I = {k: nc.dram_tensor("in_" + k, v.shape, F32, kind="ExternalInput").ap() for k, v in arrays.items()}
    out = nc.dram_tensor("out", (SEQ, D), F32, kind="ExternalOutput").ap()
    mod_dram = nc.dram_tensor("mod_rows", (DEPTH, 2, 6, D), F32, kind="Internal").ap()
    build(nc, I, out, mod_dram)
    r = run_bass_kernel_spmd(nc, [{"in_" + k: v for k, v in arrays.items()}], core_ids=[0])
    return r.results[0]["out"].reshape(1, SEQ, D)
```

```python
import math
from contextlib import ExitStack

import numpy as np
import concourse.bass as bass
from concourse import mybir

F32 = mybir.dt.float32
U32 = mybir.dt.uint32
ALU = mybir.AluOpType
ACT = mybir.ActivationFunctionType
AX = mybir.AxisListType

P = 128
D = 1024
KB = D // P
SEQ, CTX = 512, 256
DEPTH = 2
GRID_W = 64
DH = 64
NA_HEADS, NA_KC, NA_KR = 8, 16, 8
QH, KVH = 16, 4
PH, NKEYS, TOPK = 8, 128, 16
HK = PH * TOPK
ALPHA = (2 * DEPTH) ** 0.25
EPS = 1e-6
NEG = -1e30
LOWEST = -3.0e38
CT, LT = CTX // P, SEQ // P
CTX_TILES, LAT_TILES = tuple(range(CT)), tuple(range(CT, CT + LT))
SHIFT1, SCALE1, GATE1, SHIFT2, SCALE2, GATE2 = range(6)
RPW = 2 * GRID_W - 1

WCH = KB * 512
WSLOT = WCH + 512
WRING = 2
GROUP = 8
GROUPS = HK // GROUP
DRING = 4
AHEAD = 2
LAST_SLOT = 122
W_ATTN, W_TOPK = 6, 7


def constants():
    t = {}
    t["ident"] = np.eye(P, dtype=np.float32)
    a = 2 * np.pi * np.outer(np.arange(DH), np.arange(DH)) / DH
    fc = np.zeros((P, 2, P))
    for g in range(2):
        s = slice(g * DH, (g + 1) * DH)
        fc[s, 0, s], fc[s, 1, s] = np.cos(a), np.sin(a)
    t["chan_dft"] = fc.reshape(P, 2 * P).astype(np.float32)
    for name, n in (("lat", SEQ), ("ctx", CTX)):
        k = (np.outer(np.arange(n), np.arange(n)) % n) * 2 * np.pi / n
        s = 1 / math.sqrt(n * DH)
        cs = np.stack([np.cos(k) * s, -np.sin(k) * s]).reshape(2, n // P, P, n)
        t["tok_dft_" + name] = cs.transpose(2, 0, 1, 3).reshape(P, -1).astype(np.float32)
    col = np.arange(GRID_W)
    start = np.clip(col - NA_KC // 2, 0, GRID_W - NA_KC)
    ok = (col[None] >= start[:, None]) & (col[None] < start[:, None] + NA_KC)
    t["col_mask"] = np.tile(np.where(ok, 0, NEG), (2, 1)).astype(np.float32)
    q, k = np.arange(P)[:, None], np.arange(P)[None]
    band = np.zeros((P, 3, P))
    band[:, 0][k < q], band[:, 2][k > q] = NEG, NEG
    t["band_mask"] = band.reshape(P, 3 * P).astype(np.float32)
    rot = np.zeros((P, P))
    for m in range(P):
        if m % DH < DH // 2:
            rot[m + DH // 2, m] = -1
        else:
            rot[m - DH // 2, m] = 1
    t["rotate_half"] = rot.astype(np.float32)
    n_freq = DH // 4
    inv = (np.float32(10000.0) ** (-np.arange(n_freq, dtype=np.float32) / np.float32(n_freq))).astype(np.float32)
    tok = np.arange(SEQ)
    ang = np.concatenate([(tok // GRID_W).astype(np.float32)[:, None] * inv,
                          (tok % GRID_W).astype(np.float32)[:, None] * inv], -1)
    rope = np.stack([np.cos(ang), np.sin(ang)]).astype(np.float32)
    t["rope"] = np.tile(rope.transpose(2, 0, 1), (4, 1, 1)).reshape(P, 2 * SEQ).copy()
    t["iota16"] = np.tile(np.arange(TOPK, dtype=np.float32), (P, 1))
    return t


def is_lat(t):
    return t >= CT


def blocks_per_pair(T, blocks=4):
    return min(1024 // T, blocks)


def schedule():
    def attend(layer, t):
        heads = NA_HEADS if layer == 0 else QH
        return [(W_ATTN, ("attn", layer, t, k)) for k in range(heads + 2)]

    def out_proj(layer, t):
        return [(3, ("heads_out", layer, t)), (7, ("w_out", layer, t, 0)), (7, ("w_out", layer, t, 1)),
                (14, ("add_norm", layer, t))]

    def second_half(layer, t):
        jobs = [(10, ("mod2", layer, t)), (8, ("query", layer, t, 0)), (8, ("query", layer, t, 1))]
        for n in range(4):
            jobs += [(W_TOPK, ("topk", layer, t, h)) for h in (2 * n, 2 * n + 1)]
            if n + 2 < 4:
                jobs.append((8, ("query", layer, t, n + 2)))
        return jobs + [(3, ("topk_end", layer, t))]

    def ada(layer, *js):
        return [(7, ("ada", layer, j, h)) for j in js for h in range(2)]

    def mod1(layer, tiles):
        return [(10, ("mod1", layer, tiles, t)) for t in tiles]

    def project(layer, tiles, *ns):
        T, jobs = P * len(tiles), []
        for n in ns:
            if n < 3:
                per = blocks_per_pair(T)
                jobs += [(7 * per * T // 512, ("project", layer, tiles, n, b0)) for b0 in range(0, 4, per)]
            else:
                jobs += [(7, ("project", layer, tiles, n, t0)) for t0 in range(0, len(tiles), 2)]
        return jobs

    def fourier(tiles):
        per = blocks_per_pair(P * len(tiles))
        return ([(2, ("fourier", tiles, "chan", i)) for i in range(len(tiles))]
                + [(7 * len(tiles) // 2, ("fourier", tiles, "tok", b0)) for b0 in range(0, 4, per)])

    def rope(tiles):
        return [(3 * len(tiles), ("rope", tiles, n)) for n in range(3)]

    def spread(jobs):
        slots, total, at = [[] for _ in range(HK)], sum(w for w, _ in jobs), 0
        for w, job in jobs:
            slots[int((at + w / 2) * LAST_SLOT / total)].append(job)
            at += w
        return slots

    lat, ctx = LAT_TILES, CTX_TILES
    start = (ada(0, SHIFT1, SCALE1) + mod1(0, ctx) + project(0, ctx, 0) + fourier(ctx) + project(0, ctx, 1, 2, 3)
             + ada(0, GATE1) + attend(0, 0) + out_proj(0, 0) + ada(0, SHIFT2, SCALE2) + second_half(0, 0))
    background = {
        (0, 0): attend(0, 1) + out_proj(0, 1) + ada(0, GATE2) + mod1(0, lat) + project(0, lat, 0) + fourier(lat)
        + project(0, lat, 1, 2, 3) + second_half(0, 1),
        (0, 1): attend(0, 2) + out_proj(0, 2) + second_half(0, 2),
        (0, 2): ada(1, 0, 1) + attend(0, 3) + out_proj(0, 3) + second_half(0, 3),
        (0, 3): ada(1, 2, 3) + attend(0, 4) + out_proj(0, 4) + second_half(0, 4),
        (0, 4): ada(1, 4, 5) + attend(0, 5) + out_proj(0, 5) + second_half(0, 5),
        (0, 5): mod1(1, ctx) + project(1, ctx, 2, 3) + mod1(1, lat[0:2]) + project(1, lat[0:2], 0, 1, 2, 3)
        + rope(lat[0:2]) + attend(1, 2) + out_proj(1, 2) + second_half(1, 2),
        (1, 2): mod1(1, lat[2:3]) + project(1, lat[2:3], 0, 1, 2, 3) + rope(lat[2:3])
        + attend(1, 3) + out_proj(1, 3) + second_half(1, 3),
        (1, 3): mod1(1, lat[3:4]) + project(1, lat[3:4], 0, 1, 2, 3) + rope(lat[3:4])
        + attend(1, 4) + out_proj(1, 4) + second_half(1, 4),
        (1, 4): attend(1, 5) + out_proj(1, 5) + second_half(1, 5),
    }
    order = [(0, t) for t in ctx + lat] + [(1, t) for t in lat]
    phases = [(a, b, spread(background[a]) if a in background else None)
              for a, b in zip(order + [None], [None] + order)]
    return [job for _, job in start], phases, order


def build(nc, I, out, mod_dram):
    es = ExitStack()
    with es:
        def sb(name, cols, dt=F32):
            return es.enter_context(nc.sbuf_tensor(name, [P, cols], dt))

        def sem(name):
            return es.enter_context(nc.semaphore(name))

        def view(ap, k):
            return ap.rearrange("p (k n) -> p k n", k=k)

        start_jobs, phases, tile_order = schedule()
        tile_no = {lt: n for n, lt in enumerate(tile_order)}

        x_state = sb("x_state", (CT + LT) * D)
        wring = sb("wring", WRING * WSLOT)
        u_rows = view(sb("u_rows", GROUP * D), GROUP)
        v_ring = sb("v_rows", GROUP * D)
        v_rows = view(v_ring, GROUP)
        kv = sb("kv", 10240)
        h_tok = view(sb("h_tok", 2 * D), 2)
        scores_sb = view(sb("scores_sb", 1024), 2)
        work = sb("work", D)
        otok = sb("otok", D)
        probs_sb = sb("probs_sb", 2 * 768)
        probs_t = sb("probs_t", 768)
        bias_sb = sb("bias_sb", 1024)
        diags = view(sb("diags", DRING * P), DRING)
        ident = sb("ident", P)
        col_mask = sb("col_mask", GRID_W)
        band_mask = sb("band_mask", 3 * P)
        rot = sb("rot", P)
        iota16 = sb("iota16", TOPK)
        sinks, sinks_exp = sb("sinks", QH), sb("sinks_exp", QH)
        silu_c, cc, cc_exp = sb("silu_c", KB * 2), sb("cc", KB * 2), sb("cc_exp", KB * 2)
        bnst, mv = sb("bnst", 12), sb("mv", 2)
        ve, sd, rs, rt = sb("ve", 1), sb("sd", 1), sb("rs", 1), sb("rt", 1)
        negm, den, rden = sb("negm", QH), sb("den", QH), sb("rden", QH)
        acts = sb("acts", HK)
        gates = [sb(f"gates{i}", HK) for i in range(2)]
        idx_tok = [sb(f"idx_tok{i}", HK, U32) for i in range(2)]
        wts = [sb(f"wts{i}", HK) for i in range(2)]
        idx_f = sb("idx_f", HK)
        stage_u = sb("stage_u", 2 * GROUP, U32)
        stage_v = sb("stage_v", 2 * GROUP, U32)
        tiu = sb("tiu", 2 * TOPK, U32)
        bv, bpu = sb("bv", HK), sb("bpu", TOPK, U32)
        bij_u = sb("bij_u", 2 * TOPK, U32)
        tv, tif, bij, e12 = (probs_sb[:, 768 + i * 2 * TOPK:768 + (i + 1) * 2 * TOPK] for i in range(4))
        gsum = sb("gsum", PH)

        def X(t):
            return x_state[:, t * D:(t + 1) * D]

        k_lat, v_lat = view(kv[:, 0:2048], 4), view(kv[:, 2048:4096], 4)
        q_lat, fy_lat = view(kv[:, 4096:6144], 4), view(kv[:, 8192:10240], 4)
        k_ctx, v_ctx = view(kv[:, 6144:7168], 4), view(kv[:, 7168:8192], 2)
        q_ctx, fy_ctx = view(kv[:, 4096:5120], 4), view(kv[:, 2048:3072], 4)
        chan_dft = kv[:, 0:2 * P]
        q1, k1, v1 = view(kv[:, 0:2048], 8), view(kv[:, 2048:4096], 4), view(kv[:, 4096:5120], 4)
        k1_ctx, v1_ctx = view(kv[:, 5120:6144], 4), view(kv[:, 6144:6656], 2)
        at1 = kv[:, 6656:8704]
        rope_sb = view(kv[:, 8704:9728], 2)
        at0 = v_ring[:, 0:4096]
        pq = view(v_ring[:, 4096:8192], 4)
        peer_t = view(otok[:], KB)
        heads_t = view(work[:], KB)
        probs = view(probs_sb[:], 2)
        queries_t = view(probs_sb[:, 0:512], 4)
        cand, onehot, rest = probs_t[:, 0:256], probs_t[:, 256:512], probs_t[:, 512:768]
        bias = view(bias_sb[:], 2)
        mod_row = bias_sb[0:2, :]

        def modulated_t(layer, T):
            return view((at0 if layer == 0 else at1)[:, 0:KB * T], KB)

        def projected(layer, tiles, n):
            T, lat = P * len(tiles), is_lat(tiles[0])
            scale = DH ** -0.5
            if layer == 0:
                return [(q_lat if lat else q_ctx, 1.0), (q_lat if lat else q_ctx, scale),
                        (k_lat if lat else k_ctx, 1.0), (v_lat if lat else v_ctx, 1.0)][n]
            if not lat:
                return {2: (k1_ctx, 1.0), 3: (v1_ctx, 1.0)}[n]
            i = tiles[0] - CT
            c = (i % 2) * P
            return [(q1[:, 0:4, c:c + T], scale), (q1[:, 4:8, c:c + T], scale),
                    (k1[:, :, i * P:i * P + T], 1.0), (v1[:, i:i + len(tiles), :], 1.0)][n]

        def unit(layer, t, h):
            p = slice(64 * (h % 2), 64 * (h % 2) + 64)
            i = t - CT if is_lat(t) else t
            if layer == 0:
                c = slice(h * DH, (h + 1) * DH)
                vals = [v_ctx[:, m, c] for m in range(CT)]
                kc = k_ctx[p, h // 2, 0:CTX]
                if not is_lat(t):
                    return q_ctx[p, h // 2, i * P:(i + 1) * P], None, 512, kc, vals
                return (q_lat[p, h // 2, i * P:(i + 1) * P], k_lat[p, h // 2, :], 0, kc,
                        [v_lat[:, m, c] for m in range(LT)] + vals)
            g = h // (QH // KVH)
            c = slice(g * DH, (g + 1) * DH)
            t0, t1 = max(i - 1, 0), min(i + 1, LT - 1)
            q0 = (i % 2) * P
            return (q1[p, h // 2, q0:q0 + P], k1[p, g, t0 * P:(t1 + 1) * P], 512 - (t1 - t0 + 1) * P,
                    k1_ctx[p, g, 0:CTX], [v1[:, m, c] for m in range(t0, t1 + 1)] + [v1_ctx[:, m, c] for m in range(CT)])

        pairs = [es.enter_context(nc.psum_tensor(f"pair{i}", [P, 1024], F32)) for i in range(3)]
        facc = es.enter_context(nc.psum_tensor("facc", [P, 1024], F32))

        const_in, state_in, c_in = sem("const_in"), sem("state_in"), sem("c_in")
        mod_out, mod_row_ready = sem("mod_out"), sem("mod_row_ready")
        cc_exp_done, silu_done = sem("cc_exp_done"), sem("silu_done")
        chunk_in = [sem(f"chunk_in{i}") for i in range(WRING)]
        vec_free = sem("vec_free")
        pair_full = [sem(f"pair_full{i}") for i in range(3)]
        pair_free = [sem(f"pair_free{i}") for i in range(3)]
        dve_step = sem("dve_step")
        ln_var, ln_sd = sem("ln_var"), sem("ln_sd")
        h_ready = sem("h_ready")
        rope_in, roped = sem("rope_in"), sem("roped")
        bias_in, bias_free = [sem(f"bias_in{i}") for i in range(2)], sem("bias_free")
        negm_ready, exp_done, pt_ready, pv_done = sem("negm_ready"), sem("exp_done"), sem("pt_ready"), sem("pv_done")
        sink_sub, sink_exp = sem("sink_sub"), sem("sink_exp")
        o_ready = sem("o_ready")
        x_done = sem("x_done")
        scores_free = sem("scores_free")
        gate_sub, gate_exp = sem("gate_sub"), sem("gate_exp")
        idx_ready = sem("idx_ready")
        u_in = [sem(f"u_in{i}") for i in range(GROUP)]
        v_in = [sem(f"v_in{i}") for i in range(GROUP)]
        u_used, v_used = sem("u_used"), sem("v_used")
        staged = sem("staged")
        acts_ready, gelu_done, wts_ready = sem("acts_ready"), sem("gelu_done"), sem("wts_ready")
        diag_ready, f_free = sem("diag_ready"), sem("f_free")
        out_done = sem("out_done")

        taken = {}

        def take(name, eng, s, n=1):
            taken[name, s.name] = taken.get((name, s.name), 0) + n
            eng.wait_ge(s, taken[name, s.name])

        all_jobs = start_jobs + [j for _, _, slots in phases if slots for jobs in slots for j in jobs]
        rope_jobs = [job for job in all_jobs if job[0] == "rope"]

        chunks, chunk_no, chunk_freed, vecs_freed = [], {}, {}, [0]

        def chunk(name, *srcs):
            chunk_no[name] = len(chunks)
            chunks.append((name, srcs))

        def modvec(layer, t, j):
            row = 0 if is_lat(t) else 1
            return bass.AP(mod_dram.tensor, ((layer * 6 + j) * 2 + row) * D, [[0, P], [1, D]])

        def postvec(which, layer, j):
            return bass.AP(I[which].tensor, (layer * 2 + j) * D, [[0, P], [1, D]])

        def chunks_of(job):
            kind, layer = job[0], job[1]
            if kind == "ada":
                n = 2 * job[2] + job[3]
                src = bass.AP(I["ada_b"].tensor, layer * 6 * D + n * 512, [[0, 2], [1, 512]])
                chunk(job, (I["ada_w"][layer, n], 0, P), (src, WCH, 2))
            elif kind == "mod1" and job[3] == job[2][0]:
                t = job[3]
                chunk(job[:3], (modvec(layer, t, SHIFT1), 0, P), (modvec(layer, t, SCALE1), D, P))
            elif kind == "project" and job[4] == 0:
                n = job[3]
                w = I["even_w_in"][n] if layer == 0 else I["odd_w_v"] if n == 3 else I["odd_w_in"][n]
                chunk(job[:4], (w, 0, P))
            elif kind == "fourier" and job[2:] == ("chan", 0):
                chunk(job[:2], (I["tok_dft_lat" if is_lat(job[1][0]) else "tok_dft_ctx"], 0, P))
            elif kind == "w_out":
                chunk(job, (I["even_w_out" if layer == 0 else "odd_w_out"][job[3]], 0, P))
            elif kind == "add_norm":
                chunk(job, (modvec(layer, job[2], GATE1), 0, P), (postvec("post_g", layer, 0), D, P),
                      (postvec("post_b", layer, 0), 2 * D, P))
            elif kind == "mod2":
                chunk(job, (modvec(layer, job[2], SHIFT2), 0, P), (modvec(layer, job[2], SCALE2), D, P))
            elif kind == "query":
                chunk(job, (I["peer_w_q"][layer, job[3]], 0, P))
            elif kind == "close":
                chunk(job, (modvec(layer, job[2], GATE2), 0, P), (postvec("post_g", layer, 1), D, P),
                      (postvec("post_b", layer, 1), 2 * D, P))

        in_order = list(start_jobs)
        for _, v_tile, slots in phases:
            in_order += [job for jobs in slots or [] for job in jobs]
            if v_tile is not None:
                in_order.append(("close",) + v_tile)
        chunks_by = []
        for job in in_order:
            chunks_of(job)
            chunks_by.append(len(chunks))
        chunk_need, seen = [], [0] * WRING
        for n, (_, srcs) in enumerate(chunks):
            seen[n % WRING] += 16 * len(srcs)
            chunk_need.append(seen[n % WRING])

        def slot(eng, name):
            n = chunk_no[name]
            eng.wait_ge(chunk_in[n % WRING], chunk_need[n])
            return wring[:, (n % WRING) * WSLOT:(n % WRING + 1) * WSLOT]

        def vec(sl, j):
            return sl[:, j * D:(j + 1) * D]

        claimed, claims = {}, [0]

        def claim(pe, name):
            i, n = claims[0] % 3, claims[0] // 3
            claims[0] += 1
            claimed[name] = (i, n)
            if n:
                pe.wait_ge(pair_free[i], n)
            return pairs[i], pair_full[i]

        def filled(eng, name):
            i, n = claimed[name]
            eng.wait_ge(pair_full[i], n + 1)
            return pairs[i], pair_free[i], n + 1

        def emptied(eng, name):
            i, n = claimed[name]
            eng.wait_ge(pair_free[i], n + 1)

        block = es.enter_context(nc.Block())

        @block.tensor
        def _(pe):
            def mm(o, lhsT, rhs, start, stop):
                return nc.tensor.matmul(o, lhsT=lhsT, rhs=rhs, start=start, stop=stop, skip_group_check=True)

            def last_use(name):
                chunk_freed[name] = pair_full[(claims[0] - 1) % 3], (claims[0] - 1) // 3 + 1

            def weights(name, cols=512):
                return view(slot(pe, name)[:, 0:KB * cols], KB)

            def transposes(name, src, blocks):
                pair, full = claim(pe, name)
                for k in range(blocks):
                    last = nc.tensor.transpose(pair[:, k * P:(k + 1) * P], src[:, k * P:(k + 1) * P], ident[:])
                last.then_inc(full, 1)

            def ada(job):
                _, layer, j, h = job
                sc = silu_c[:].rearrange("p (k c) -> p k c", k=KB)
                if h == 0:
                    claim(pe, job[:3])
                i, n = claimed[job[:3]]
                w = weights(job)
                for k in range(KB):
                    last = mm(pairs[i][0:2, h * 512:(h + 1) * 512], sc[:, k, :], w[:, k, :], k == 0, k == KB - 1)
                chunk_freed[job] = pair_free[i], n + 1
                if h:
                    last.then_inc(pair_full[i], 1)

            def mod1(job):
                take("pe", pe, h_ready)
                transposes(job, work[:], KB)

            def project(job):
                _, layer, tiles, n, first = job
                T = P * len(tiles)
                for t in tiles:
                    emptied(pe, ("mod1", layer, tiles, t))
                src = modulated_t(layer, T)
                pair, full = claim(pe, job)
                if n < 3:
                    w = weights(job[:4])
                    for j in range(blocks_per_pair(T)):
                        for k in range(KB):
                            last = mm(pair[:, j * T:(j + 1) * T], w[:, k, (first + j) * P:(first + j + 1) * P],
                                      src[:, k, :], k == 0, k == KB - 1)
                else:
                    width = 512 if layer == 0 else KVH * DH
                    w = weights(job[:4], width)
                    for j in range(min(2, len(tiles))):
                        for k in range(KB):
                            last = mm(pair[:, j * 512:j * 512 + width], src[:, k, (first + j) * P:(first + j + 1) * P],
                                      w[:, k, :], k == 0, k == KB - 1)
                last.then_inc(full, 1)
                last_use(job[:4])

            def fourier(job):
                _, tiles, stage, first = job
                nt, T = len(tiles), P * len(tiles)
                ft = projected(0, tiles, 0)[0]
                if job[2:] == ("chan", 0):
                    for b0 in range(0, 4, blocks_per_pair(T)):
                        emptied(pe, ("project", 0, tiles, 0, b0))
                if job[2:] == ("tok", 0):
                    for i in range(nt):
                        emptied(pe, ("fourier", tiles, "chan", i))
                pair, full = claim(pe, job)
                if stage == "chan":
                    for b in range(4):
                        last = mm(pair[:, b * 256:(b + 1) * 256], ft[:, b, first * P:(first + 1) * P], chan_dft,
                                  True, True)
                else:
                    w = view(slot(pe, job[:2])[:, 0:2 * nt * T], 2 * nt)
                    for j in range(blocks_per_pair(T)):
                        for k in range(2 * nt):
                            c = (first + j) * 256 + (k // nt) * P
                            last = mm(pair[:, j * T:(j + 1) * T], pq[:, k % nt, c:c + P], w[:, k, :],
                                      k == 0, k == 2 * nt - 1)
                    last_use(job[:2])
                last.then_inc(full, 1)

            def rope(job):
                _, tiles, n = job
                T = P * len(tiles)
                dst, _ = projected(1, tiles, n)
                for b0 in range(0, 4, blocks_per_pair(T)):
                    emptied(pe, ("project", 1, tiles, n, b0))
                pair, full = claim(pe, job)
                for b in range(4):
                    last = mm(pair[:, b * T:(b + 1) * T], rot[:], dst[:, b, :], True, True)
                last.then_inc(full, 1)

            def attn(job):
                _, layer, t, k = job
                if k == 0 and layer == 0:
                    tiles = LAT_TILES if is_lat(t) else CTX_TILES
                    for n in (1, 2):
                        for b0 in range(0, 4, blocks_per_pair(P * len(tiles))):
                            emptied(pe, ("project", 0, tiles, n, b0))
                    for t0 in range(0, len(tiles), 2):
                        emptied(pe, ("project", 0, tiles, 3, t0))
                if k == 0 and layer == 1:
                    for tiles in (CTX_TILES, LAT_TILES[0:2], LAT_TILES[2:3], LAT_TILES[3:4]):
                        if ("project", 1, tiles, 3, 0) in claimed:
                            emptied(pe, ("project", 1, tiles, 3, 0))
                        if ("rope", tiles, 2) in claimed:
                            pe.wait_ge(roped, rope_jobs.index(("rope", tiles, 2)) + 1)
                    emptied(pe, ("project", 1, CTX_TILES, 2, 0))
                heads = NA_HEADS if layer == 0 else QH
                if k >= 2:
                    _, _, lo, _, vals = unit(layer, t, k - 2)
                    i, _ = claimed["t", layer, t, k - 2]
                    take("pe", pe, pt_ready)
                    for n, b in enumerate(range(lo // P, 6)):
                        last = mm(pairs[i][:, 768:768 + DH], probs_t[:, b * P:(b + 1) * P], vals[n], n == 0, b == 5)
                    last.then_inc(pv_done, 1)
                if 1 <= k <= heads:
                    h = k - 1
                    lo = unit(layer, t, h)[2]
                    take("pe", pe, exp_done)
                    pair, full = claim(pe, ("t", layer, t, h))
                    for b in range(lo // P, 6):
                        last = nc.tensor.transpose(pair[:, b * P:(b + 1) * P], probs[:, h % 2, b * P:(b + 1) * P], ident[:])
                    last.then_inc(full, 1)
                if k < heads:
                    q, kl, lo, kc, _ = unit(layer, t, k)
                    pair, full = claim(pe, ("s", layer, t, k))
                    if kl is not None:
                        mm(pair[:, lo:512], q, kl, True, True)
                    mm(pair[:, 512:768], q, kc, True, True).then_inc(full, 1)

            def heads_out(job):
                take("pe", pe, o_ready)
                transposes(job, otok[:], 4 if job[1] == 0 else 8)

            def w_out(job):
                _, layer, t, n = job
                lat = is_lat(t)
                i = t - CT if lat else t
                emptied(pe, ("heads_out", layer, t))
                if layer == 0 and i == 0:
                    for b0 in range(0, 4, 2 if lat else 4):
                        emptied(pe, ("fourier", LAT_TILES if lat else CTX_TILES, "tok", b0))
                fy = fy_lat if lat else fy_ctx
                if layer == 0:
                    blocks = [fy[:, b, i * P:(i + 1) * P] for b in range(4)] + [heads_t[:, b, :] for b in range(4)]
                else:
                    blocks = [heads_t[:, b, :] for b in range(8)]
                if n == 0:
                    claim(pe, job[:3])
                j, c = claimed[job[:3]]
                w = weights(job)
                for k in range(KB):
                    last = mm(pairs[j][:, n * 512:(n + 1) * 512], blocks[k], w[:, k, :], k == 0, k == KB - 1)
                chunk_freed[job] = pair_full[j], c + 1
                if n:
                    last.then_inc(pair_full[j], 1)

            def mod2(job):
                _, layer, t = job
                take("pe", pe, h_ready)
                transposes(job, h_tok[:, tile_no[layer, t] % 2, :], KB)

            def query(job):
                _, layer, t, n = job
                if n == 0:
                    emptied(pe, ("mod2", layer, t))
                sl = slot(pe, job)
                w = view(sl[:, 0:WCH], KB)
                pair, full = claim(pe, job)
                for b in range(4):
                    for k in range(KB):
                        last = mm(pair[:, b * P:(b + 1) * P], w[:, k, b * P:(b + 1) * P], peer_t[:, k, :],
                                  k == 0, k == KB - 1)
                last.then_inc(full, 1)
                emptied(pe, job)
                pair, full = claim(pe, job + ("scores",))
                for b in range(4):
                    last = mm(pair[:, b * P:(b + 1) * P], queries_t[:, b, :], sl[:, WCH + b * P:WCH + (b + 1) * P],
                              True, True)
                last.then_inc(full, 1)
                last_use(job)

            do = dict(ada=ada, mod1=mod1, project=project, fourier=fourier, rope=rope, attn=attn,
                      heads_out=heads_out, w_out=w_out, mod2=mod2, query=query)

            def accumulate(group, g, r, start):
                pe.wait_ge(v_in[r], g * 16 + 16 * (group + 1))
                pe.wait_ge(diag_ready, g * GROUP + (group * GROUP + r + 1))
                for c in range(2):
                    last = mm(facc[:, c * 512:(c + 1) * 512], diags[:, r % DRING, :],
                              v_rows[:, r, c * 512:(c + 1) * 512], start, False)
                last.then_inc(v_used, 1)

            pe.wait_ge(const_in, 16 * 8)
            take("pe", pe, silu_done)
            for job in start_jobs:
                if job[0] in do:
                    do[job[0]](job)
            for _, v_tile, slots in phases:
                first = tile_no[v_tile] * GROUPS if v_tile is not None else 0
                if v_tile is not None and tile_no[v_tile]:
                    pe.wait_ge(f_free, tile_no[v_tile])
                if slots is None:
                    if v_tile is not None:
                        for r in range(GROUP):
                            accumulate(first, 0, r, r == 0)
                        with pe.Fori(1, GROUPS) as g:
                            for r in range(GROUP):
                                accumulate(first, g, r, False)
                    continue
                for s, jobs in enumerate(slots):
                    if v_tile is not None:
                        accumulate(first + s // GROUP, 0, s % GROUP, s == 0)
                    for job in jobs:
                        if job[0] in do:
                            do[job[0]](job)

        @block.scalar
        def _(act):
            def evac(name, dst, src, scale=1.0):
                pair, free, n = filled(act, name)
                nc.scalar.activation(dst, src(pair), ACT.Copy, scale=scale).then_inc(free, 1)

            def sqrt_of_variance():
                take("act", act, ln_var)
                nc.scalar.activation(sd[:], ve[:], ACT.Sqrt).then_inc(ln_sd, 1)

            def mod1(job):
                _, layer, tiles, t = job
                at, i = modulated_t(layer, P * len(tiles)), tiles.index(t)
                sqrt_of_variance()
                evac(job, at[:, :, i * P:(i + 1) * P], lambda pair: view(pair[:], KB))

            def project(job):
                _, layer, tiles, n, first = job
                T = P * len(tiles)
                dst, scale = projected(layer, tiles, n)
                if n < 3:
                    per = blocks_per_pair(T)
                    evac(job, dst[:, first:first + per, :], lambda pair: view(pair[:, 0:per * T], per), scale)
                else:
                    width, per = (512 if layer == 0 else KVH * DH), min(2, len(tiles))
                    evac(job, dst[:, first:first + per, :], lambda pair: view(pair[:], 2)[:, 0:per, 0:width])

            def fourier(job):
                _, tiles, stage, first = job
                if stage == "chan":
                    evac(job, pq[:, first, :], lambda pair: pair[:])
                else:
                    fy, per = (fy_lat if is_lat(tiles[0]) else fy_ctx), blocks_per_pair(P * len(tiles))
                    evac(job, fy[:, first:first + per, :], lambda pair: view(pair[:], per))

            units_done = [0]

            def attn(job):
                _, layer, t, k = job
                heads = NA_HEADS if layer == 0 else QH
                lo = unit(layer, t, 0)[2]
                if 1 <= k <= heads:
                    i, n = claimed["t", layer, t, k - 1]
                    act.wait_ge(pair_full[i], n + 1)
                    if units_done[0]:
                        act.wait_ge(pv_done, units_done[0])
                    units_done[0] += 1
                    nc.scalar.activation(probs_t[:, lo:768], pairs[i][:, lo:768], ACT.Copy).then_inc(pt_ready, 1)
                if k < heads:
                    take("act", act, negm_ready)
                    i, n = claimed["s", layer, t, k]
                    nc.scalar.activation(probs[:, k % 2, lo:768], pairs[i][:, lo:768], ACT.Exp,
                                         bias=negm[:, k:k + 1], accum_out=den[:, k:k + 1]).then_inc(pair_free[i], 1)
                    act.wait_ge(pair_free[i], n + 1)
                    nc.scalar.sem_inc(exp_done, 1)

            def heads_out(job):
                blocks = 4 if job[1] == 0 else 8
                if job[1] == 1:
                    take("act", act, sink_sub)
                    nc.scalar.activation(sinks_exp[:], sinks_exp[:], ACT.Exp).then_inc(sink_exp, 1)
                evac(job, heads_t[:, 0:blocks, :], lambda pair: view(pair[:, 0:blocks * P], blocks))

            def mod2(job):
                sqrt_of_variance()
                evac(job, peer_t, lambda pair: view(pair[:], KB))

            queries_done = [0]

            def query(job):
                n = job[3]
                evac(job, queries_t, lambda pair: view(pair[:, 0:512], 4))
                if queries_done[0] >= 2:
                    act.wait_ge(scores_free, queries_done[0] - 1)
                queries_done[0] += 1
                evac(job + ("scores",), scores_sb[:, n % 2, :], lambda pair: pair[:, 0:512])

            def topk_end(job):
                b = tile_no[job[1:]] % 2
                take("act", act, gate_sub)
                nc.scalar.activation(gates[b][:], gates[b][:], ACT.Exp).then_inc(gate_exp, 1)

            do = dict(mod1=mod1, project=project, fourier=fourier, attn=attn, heads_out=heads_out,
                      add_norm=lambda job: sqrt_of_variance(), mod2=mod2, query=query, topk_end=topk_end)

            def diagonal(b, first, s, g=None):
                need = first + s + 1 - DRING + GROUP
                act.wait_ge(v_used, need if g is None else g * GROUP + need)
                scale = wts[b][:, s:s + 1] if g is None else wts[b][:, bass.ds(g * GROUP + s, 1)]
                nc.scalar.activation(diags[:, s % DRING, :], ident[:], ACT.Copy, scale=scale).then_inc(diag_ready, 1)

            act.wait_ge(c_in, 16)
            nc.scalar.activation(cc_exp[:], cc[:], ACT.Exp, scale=-1.0).then_inc(cc_exp_done, 1)
            for job in start_jobs:
                if job[0] in do:
                    do[job[0]](job)
            for u_tile, v_tile, slots in phases:
                if v_tile is not None:
                    n = tile_no[v_tile]
                    first = n * HK
                    act.wait_ge(wts_ready, n + 1)
                if slots is None:
                    if v_tile is not None:
                        with act.Fori(0, GROUPS) as g:
                            for r in range(GROUP):
                                diagonal(n % 2, first, r, g)
                else:
                    if v_tile is not None:
                        for s in range(AHEAD):
                            diagonal(n % 2, first, s)
                    for s, jobs in enumerate(slots):
                        if v_tile is not None and s + AHEAD < HK:
                            diagonal(n % 2, first, s + AHEAD)
                        for job in jobs:
                            if job[0] in do:
                                do[job[0]](job)
                if u_tile is not None:
                    take("act", act, acts_ready)
                    nc.scalar.activation(acts[:], acts[:], ACT.Gelu).then_inc(gelu_done, 1)
                if v_tile is not None:
                    sqrt_of_variance()

        @block.vector
        def _(v):
            V = nc.vector
            counts = {}

            def signal(ins, s):
                counts[s.name] = counts.get(s.name, 0) + 1
                ins.then_inc(s, 1)
                v.wait_ge(s, counts[s.name])

            def step(ins):
                signal(ins, dve_step)

            def last_read(ins, free, count):
                ins.then_inc(free, 1)
                v.wait_ge(free, count)

            def statistics(t):
                for h in range(2):
                    step(V.bn_stats(bnst[:, 6 * h:6 * h + 6], X(t)[:, h * 512:(h + 1) * 512]))
                step(V.bn_aggr(mv[:], bnst[:]))
                signal(V.tensor_scalar(ve[:], mv[:, 1:2], EPS, None, ALU.add), ln_var)
                take("dve", v, ln_sd)
                step(V.reciprocal(rs[:], sd[:]))
                step(V.tensor_tensor(rt[:], rs[:], rs[:], ALU.mult))
                step(V.tensor_tensor(rt[:], rt[:], ve[:], ALU.mult))
                step(V.tensor_scalar(rt[:], rt[:], -0.5, 1.5, ALU.mult, ALU.add))
                step(V.tensor_tensor(rs[:], rs[:], rt[:], ALU.mult))

            def normalised(t, dst, scale, shift):
                step(V.tensor_scalar(dst, X(t), mv[:, 0:1], rs[:], ALU.subtract, ALU.mult))
                step(V.tensor_tensor(dst, dst, scale, ALU.mult))
                return V.tensor_tensor(dst, dst, shift, ALU.add)

            def free(name):
                vecs_freed[0] += 1
                chunk_freed[name] = vec_free, vecs_freed[0]
                V.sem_inc(vec_free, 1)

            rows_made = [0]

            def ada(job):
                _, layer, j, half = job
                if half == 0:
                    return
                pair, fr, n = filled(v, job[:3])
                if rows_made[0]:
                    v.wait_ge(mod_out, 16 * rows_made[0])
                rows_made[0] += 1
                one = 1.0 if j in (SCALE1, SCALE2) else 0.0
                for h in range(2):
                    c = slice(h * 512, (h + 1) * 512)
                    sl = slot(v, job[:3] + (h,))
                    ins = V.scalar_tensor_tensor(mod_row[:, c], pair[0:2, c], one, sl[0:2, WCH:WCH + 512],
                                                 ALU.add, ALU.add)
                    if h == 0:
                        step(ins)
                    else:
                        last_read(ins, fr, n)
                V.sem_inc(mod_row_ready, 1)

            def mod1(job):
                _, layer, tiles, t = job
                i = tiles.index(t)
                statistics(t)
                sl = slot(v, job[:3])
                if i:
                    filled(v, job[:3] + (tiles[i - 1],))
                signal(normalised(t, work[:], vec(sl, 1), vec(sl, 0)), h_ready)
                if t == tiles[-1]:
                    free(job[:3])

            def rope(job):
                _, tiles, n = job
                T, i = P * len(tiles), tiles[0] - CT
                v.wait_ge(rope_in, 16)
                wide = [P, 4, T]
                cos, sin = (rope_sb[:, m, i * P:i * P + T].unsqueeze(1).to_broadcast(wide) for m in range(2))
                a, b = view(work[:, 0:4 * T], 4), view(otok[:, 0:4 * T], 4)
                dst, _ = projected(1, tiles, n)
                pair, fr, cnt = filled(v, job)
                last_read(V.tensor_tensor(a, view(pair[:, 0:4 * T], 4), sin, ALU.mult), fr, cnt)
                step(V.tensor_tensor(b, dst, cos, ALU.mult))
                signal(V.tensor_tensor(dst, a, b, ALU.add), roped)

            biases = [0]

            def attn(job):
                _, layer, t, k = job
                i = t - CT
                if k >= 2:
                    take("dve", v, pv_done)
                    j, n = claimed["t", layer, t, k - 2]
                    last_read(V.tensor_copy(otok[:, (k - 2) * DH:(k - 1) * DH], pairs[j][:, 768:768 + DH]),
                              pair_free[j], n + 1)
                if k < (NA_HEADS if layer == 0 else QH):
                    lo = unit(layer, t, k)[2]
                    pair, _, _ = filled(v, ("s", layer, t, k))
                    local, negm_k = pair[:, lo:512], negm[:, k:k + 1]
                    if layer == 0 and is_lat(t):
                        b = biases[0] % 2
                        v.wait_ge(bias_in[b], 32 * (biases[0] // 2 + 1))
                        biases[0] += 1
                        signal(V.tensor_tensor(local, local, bias[:, b, :], ALU.add), bias_free)
                        wide = [P, NA_KR, GRID_W]
                        step(V.tensor_tensor(view(local, NA_KR), view(local, NA_KR),
                                             col_mask[:].unsqueeze(1).to_broadcast(wide), ALU.add))
                    if layer == 1:
                        m0 = (max(i - 1, 0) - i + 1) * P
                        step(V.tensor_tensor(local, local, band_mask[:, m0:m0 + 512 - lo], ALU.add))
                        step(V.tensor_reduce(negm_k, pair[:, lo:768], AX.X, ALU.max))
                        signal(V.tensor_scalar(negm_k, negm_k, sinks[:, k:k + 1], -1.0, ALU.max, ALU.mult), negm_ready)
                    else:
                        signal(V.tensor_reduce(negm_k, pair[:, lo:768], AX.X, ALU.max, negate=True), negm_ready)

            def heads_out(job):
                heads = NA_HEADS if job[1] == 0 else QH
                r = slice(0, heads)
                if job[1] == 1:
                    signal(V.tensor_tensor(sinks_exp[:], sinks[:], negm[:], ALU.add), sink_sub)
                    take("dve", v, sink_exp)
                    step(V.tensor_tensor(den[:], den[:], sinks_exp[:], ALU.add))
                step(V.reciprocal(rden[:, r], den[:, r]))
                o = view(otok[:, 0:heads * DH], heads)
                signal(V.tensor_tensor(o, o, rden[:, r].unsqueeze(2).to_broadcast([P, heads, DH]), ALU.mult), o_ready)

            def add_norm(job):
                _, layer, t = job
                pair, fr, n = filled(v, ("w_out", layer, t))
                sl = slot(v, job)
                last_read(V.tensor_tensor(work[:], pair[:], vec(sl, 0), ALU.mult), fr, n)
                step(V.scalar_tensor_tensor(X(t), X(t), ALPHA, work[:], ALU.mult, ALU.add))
                statistics(t)
                step(normalised(t, X(t), vec(sl, 1), vec(sl, 2)))
                free(job)

            def mod2(job):
                _, layer, t = job
                statistics(t)
                sl = slot(v, job)
                signal(normalised(t, h_tok[:, tile_no[layer, t] % 2, :], vec(sl, 1), vec(sl, 0)), h_ready)
                free(job)

            def top16(vals, idxs, src, n):
                step(V.max(vals[:, 0:8], src))
                V.max_index(idxs[:, 0:8], vals[:, 0:8], src)
                step(V.match_replace(rest[:, 0:n], vals[:, 0:8], src, LOWEST))
                step(V.max(vals[:, 8:16], rest[:, 0:n]))
                step(V.max_index(idxs[:, 8:16], vals[:, 8:16], rest[:, 0:n]))

            def topk(job):
                _, layer, t, h = job
                if h % 2 == 0:
                    emptied(v, ("query", layer, t, h // 2, "scores"))
                for p in range(2):
                    c = (2 * (h % 2) + p) * P
                    src = scores_sb[:, (h // 2) % 2, c:c + P]
                    top16(tv[:, p * TOPK:(p + 1) * TOPK], tiu[:, p * TOPK:(p + 1) * TOPK], src, P)
                if h % 2:
                    V.sem_inc(scores_free, 1)
                wide = [P, TOPK, TOPK]
                cands, oh = view(cand, TOPK), view(onehot, TOPK)
                V.tensor_copy(tif, tiu[:])
                step(V.tensor_tensor(cands, tv[:, 0:TOPK].unsqueeze(2).to_broadcast(wide),
                                     tv[:, TOPK:].unsqueeze(1).to_broadcast(wide), ALU.add))
                top16(bv[:, h * TOPK:(h + 1) * TOPK], bpu[:], cand, TOPK * TOPK)
                V.tensor_scalar(bij_u[:, 0:TOPK], bpu[:], 4, None, ALU.logical_shift_right)
                step(V.tensor_scalar(bij_u[:, TOPK:], bpu[:], 15, None, ALU.bitwise_and))
                step(V.tensor_copy(bij, bij_u[:]))
                for p in range(2):
                    sl = slice(p * TOPK, (p + 1) * TOPK)
                    step(V.tensor_tensor(oh, bij[:, sl].unsqueeze(2).to_broadcast(wide),
                                         iota16[:].unsqueeze(1).to_broadcast(wide), ALU.is_equal))
                    step(V.tensor_tensor(oh, oh, tif[:, sl].unsqueeze(1).to_broadcast(wide), ALU.mult))
                    step(V.tensor_reduce(e12[:, sl], oh, AX.X, ALU.add))
                step(V.scalar_tensor_tensor(idx_f[:, h * TOPK:(h + 1) * TOPK], e12[:, 0:TOPK], float(NKEYS),
                                            e12[:, TOPK:], ALU.mult, ALU.add))

            def topk_end(job):
                b = tile_no[job[1:]] % 2
                wide = [P, PH, TOPK]
                hv, gv = view(bv[:], PH), view(gates[b][:], PH)
                signal(V.tensor_copy(idx_tok[b][:], idx_f[:]), idx_ready)
                signal(V.tensor_tensor(gv, hv, hv[:, :, 0:1].to_broadcast(wide), ALU.subtract), gate_sub)
                take("dve", v, gate_exp)
                step(V.tensor_reduce(gsum[:], gv, AX.X, ALU.add))
                step(V.reciprocal(gsum[:], gsum[:]))
                step(V.tensor_tensor(gv, gv, gsum[:].unsqueeze(2).to_broadcast(wide), ALU.mult))

            do = dict(ada=ada, mod1=mod1, rope=rope, attn=attn, heads_out=heads_out, add_norm=add_norm, mod2=mod2,
                      topk=topk, topk_end=topk_end)

            def dot(tile, s, g=None):
                n, r = tile_no[tile], s % GROUP
                landed = 16 * (n * GROUPS + s // GROUP + 1)
                v.wait_ge(u_in[r], landed if g is None else g * 16 + landed)
                a = acts[:, s:s + 1] if g is None else acts[:, bass.ds(g * GROUP + s, 1)]
                V.scalar_tensor_tensor(u_rows[:, r, :], u_rows[:, r, :], 1.0, h_tok[:, n % 2, :], ALU.mult, ALU.mult,
                                       accum_out=a).then_inc(u_used, 1)

            V.sem_inc(u_used, GROUP)
            v.wait_ge(const_in, 16 * 8)
            take("dve", v, cc_exp_done)
            step(V.tensor_scalar(silu_c[:], cc_exp[:], 1.0, None, ALU.add))
            step(V.reciprocal(silu_c[:], silu_c[:]))
            signal(V.tensor_tensor(silu_c[:], silu_c[:], cc[:], ALU.mult), silu_done)
            v.wait_ge(state_in, 32)
            for job in start_jobs:
                if job[0] in do:
                    do[job[0]](job)
            for u_tile, v_tile, slots in phases:
                if slots is None and u_tile is not None:
                    with v.Fori(0, GROUPS) as g:
                        for r in range(GROUP):
                            dot(u_tile, r, g)
                for s, jobs in enumerate(slots or []):
                    dot(u_tile, s)
                    for job in jobs:
                        if job[0] in do:
                            do[job[0]](job)
                if u_tile is not None:
                    v.wait_ge(u_used, GROUP + HK * (tile_no[u_tile] + 1))
                    V.sem_inc(acts_ready, 1)
                    b = tile_no[u_tile] % 2
                    take("dve", v, gelu_done)
                    signal(V.tensor_tensor(wts[b][:], acts[:], gates[b][:], ALU.mult), wts_ready)
                if v_tile is not None:
                    layer, t = v_tile
                    n = tile_no[v_tile] + 1
                    sl = slot(v, ("close",) + v_tile)
                    v.wait_ge(v_used, GROUP + HK * n)
                    signal(V.tensor_tensor(work[:], facc[:], vec(sl, 0), ALU.mult), f_free)
                    step(V.scalar_tensor_tensor(X(t), X(t), ALPHA, work[:], ALU.mult, ALU.add))
                    statistics(t)
                    signal(normalised(t, X(t), vec(sl, 1), vec(sl, 2)), x_done)
                    free(("close",) + v_tile)

        @block.gpsimd
        def _(pool):
            need_u = es.enter_context(pool.register("need_u"))
            need_v = es.enter_context(pool.register("need_v"))
            need_staged = es.enter_context(pool.register("need_staged"))
            pool.sem_inc(v_used, GROUP)
            pool.reg_mov(need_u, 1)
            pool.reg_mov(need_v, 1)
            staged_before = 0
            for u_tile, v_tile, _ in phases:
                if u_tile is not None:
                    pool.wait_ge(idx_ready, tile_no[u_tile] + 1)
                both = (u_tile is not None) + (v_tile is not None)
                pool.reg_mov(need_staged, staged_before + both)
                staged_before += both * GROUPS
                with pool.Fori(0, GROUPS // 2) as g:
                    for half in range(2):
                        cols = slice(half * GROUP, (half + 1) * GROUP)
                        src = bass.ds(g * 2 * GROUP + half * GROUP, GROUP)
                        if u_tile is not None:
                            nc.gpsimd.tensor_copy(stage_u[:, cols], idx_tok[tile_no[u_tile] % 2][:, src]).then_inc(staged, 1)
                        if v_tile is not None:
                            nc.gpsimd.tensor_copy(stage_v[:, cols], idx_tok[tile_no[v_tile] % 2][:, src]).then_inc(staged, 1)
                        pool.wait_ge(staged, need_staged)
                        pool.reg_add(need_staged, need_staged, both)
                        for r in range(GROUP):
                            j = half * GROUP + r
                            if u_tile is not None:
                                pool.wait_ge(u_used, need_u)
                                pool.reg_add(need_u, need_u, 1)
                                pool.indirect_dma_start(
                                    u_rows[:, r, :], None, I[f"peer_u{u_tile[0]}"],
                                    bass.IndirectOffsetOnAxis(ap=stage_u[:, j:j + 1], axis=0)).then_inc(u_in[r], 16)
                            if v_tile is not None:
                                pool.wait_ge(v_used, need_v)
                                pool.reg_add(need_v, need_v, 1)
                                pool.indirect_dma_start(
                                    v_rows[:, r, :], None, I[f"peer_v{v_tile[0]}"],
                                    bass.IndirectOffsetOnAxis(ap=stage_v[:, j:j + 1], axis=0)).then_inc(v_in[r], 16)

        @block.sync
        def _(sp):
            sp.dma_start(cc[:], I["cc"]).then_inc(c_in, 16)
            for dst, name in ((ident[:], "ident"), (chan_dft, "chan_dft"), (col_mask[:], "col_mask"),
                              (band_mask[:], "band_mask"), (rot[:], "rotate_half"), (iota16[:], "iota16")):
                sp.dma_start(dst, I[name]).then_inc(const_in, 16)
            for dst in (sinks, sinks_exp):
                sp.dma_start(dst[:], bass.AP(I["gqa_sink"].tensor, 0, [[0, P], [1, QH]])).then_inc(const_in, 16)
            rows_stored, loaded, biases = [0], [0], [0]

            def load(n):
                name, srcs = chunks[n]
                if n >= WRING:
                    sp.wait_ge(*chunk_freed[chunks[n - WRING][0]])
                for src, col, rows in srcs:
                    a = (n % WRING) * WSLOT + col
                    sp.dma_start(wring[0:rows, a:a + src.shape[-1]], src).then_inc(chunk_in[n % WRING], 16)

            def load_to(n):
                while loaded[0] < min(n, len(chunks)):
                    load(loaded[0])
                    loaded[0] += 1

            mod_rows = [job[:3] for job in all_jobs if job[0] == "ada" and job[3] == 1]

            def rows_needed(n):
                js = {"mod1": SCALE1, "add_norm": GATE1, "mod2": SCALE2, "close": GATE2}
                return max([0] + [mod_rows.index(("ada", name[1], js[name[0]])) + 1
                                  for name, _ in chunks[:n] if name[0] in js])

            def ahead(n):
                n += WRING
                while rows_needed(n) > rows_stored[0]:
                    n -= 1
                load_to(n)

            def load_bias(t, h):
                if biases[0] >= 2:
                    sp.wait_ge(bias_free, biases[0] - 1)
                for a in range(2):
                    c = (NA_KR - 2 * (t - CT) - a) * GRID_W
                    sp.dma_start(bias[64 * a:64 * a + 64, biases[0] % 2, :],
                                 I["rpb"][h][:, c:c + NA_KR * GRID_W]).then_inc(bias_in[biases[0] % 2], 16)
                biases[0] += 1

            load_to(1)
            sp.dma_start(view(x_state[:, 0:CT * D], CT), I["ctx"].rearrange("(t p) d -> p t d", p=P)).then_inc(state_in, 16)
            sp.dma_start(view(x_state[:, CT * D:], LT), I["x"].rearrange("(t p) d -> p t d", p=P)).then_inc(state_in, 16)
            for job, n in zip(in_order, chunks_by):
                load_to(n)
                if job[0] == "ada" and job[3] == 1:
                    sp.wait_ge(mod_row_ready, rows_stored[0] + 1)
                    dst = bass.AP(mod_dram.tensor, (job[1] * 6 + job[2]) * 2 * D, [[D, 2], [1, D]])
                    sp.dma_start(dst, mod_row).then_inc(mod_out, 16)
                    rows_stored[0] += 1
                    sp.wait_ge(mod_out, 16 * rows_stored[0])
                if job[0] == "attn" and job[1] == 0 and is_lat(job[2]):
                    if job[3] == 0:
                        load_bias(job[2], 0)
                    if job[3] + 1 < NA_HEADS:
                        load_bias(job[2], job[3] + 1)
                if job == ("mod1", 1, CTX_TILES, 0):
                    sp.wait_ge(idx_ready, tile_no[0, CT + LT - 1] + 1)
                    sp.dma_start(view(kv[:, 8704:9728], 2), I["rope"].rearrange("p (k n) -> p k n", k=2)).then_inc(rope_in, 16)
                ahead(n)
            for i in range(LT):
                sp.wait_ge(x_done, CT + LT + i + 1)
                sp.dma_start(out[i * P:(i + 1) * P, :], X(CT + i)).then_inc(out_done, 16)
            sp.wait_ge(out_done, 16 * LT)


def chunked(w, cols=512):
    n = w.shape[1] // cols
    return np.ascontiguousarray(w.reshape(KB, P, n, cols).transpose(2, 1, 0, 3).reshape(n, P, KB * cols))


def layout(inputs):
    a = {k: np.asarray(v) for k, v in inputs.items()}
    t = constants()
    t["x"] = a["x"][0]
    t["ctx"] = a["ctx"][0]
    t["cc"] = np.stack([a["c"][0].reshape(KB, P), a["c_ctx"].reshape(KB, P)], -1).transpose(1, 0, 2).reshape(P, KB * 2)
    t["ada_w"] = np.stack([chunked(a["ada_w"][l]) for l in range(DEPTH)])
    t["ada_b"] = a["ada_b"]
    t["post_g"], t["post_b"] = a["post_ln_g"], a["post_ln_b"]
    t["even_w_in"], t["even_w_out"] = chunked(a["even_w_in"][0]), chunked(a["even_w_out"][0])
    w = a["odd_w_in"][0]
    kw = w[:, QH * DH:(QH + KVH) * DH].reshape(D, KVH, 1, DH)
    kw = np.concatenate([kw, kw], 2).reshape(D, 512)
    t["odd_w_in"] = np.concatenate([chunked(w[:, :QH * DH]), chunked(kw)])
    t["odd_w_v"] = chunked(w[:, (QH + KVH) * DH:], 256)[0]
    t["odd_w_out"] = chunked(a["odd_w_out"][0])
    t["gqa_sink"] = a["gqa_sink"]
    rpb = a["na_rpb"][0]
    pad = np.zeros((NA_HEADS, 17, RPW), np.float32)
    c0 = GRID_W - NA_KC
    pad[:, 1:16, c0:c0 + 2 * NA_KC - 1] = rpb
    t["rpb"] = np.stack([pad[:, :, GRID_W - 1 - c:RPW - c] for c in range(GRID_W)], 1).reshape(NA_HEADS, GRID_W, -1)
    wq = np.stack([chunked(a["peer_w_q"][l]) for l in range(DEPTH)])
    sk = a["peer_sub_keys"].transpose(0, 4, 1, 2, 3).reshape(DEPTH, P, 4, 512).transpose(0, 2, 1, 3)
    t["peer_w_q"] = np.concatenate([wq, sk], -1)
    for l in range(DEPTH):
        t[f"peer_u{l}"], t[f"peer_v{l}"] = a["peer_u"][l], a["peer_v"][l]
    return {k: np.ascontiguousarray(v) for k, v in t.items()}


def kernel(**inputs):
    import concourse.bacc as bacc
    from concourse.bass_utils import run_bass_kernel_spmd

    nc = bacc.Bacc("TRN2", target_bir_lowering=False, num_devices=1)
    arrays = layout(inputs)
    I = {k: nc.dram_tensor("in_" + k, v.shape, F32, kind="ExternalInput").ap() for k, v in arrays.items()}
    out = nc.dram_tensor("out", (SEQ, D), F32, kind="ExternalOutput").ap()
    mod_dram = nc.dram_tensor("mod_rows", (DEPTH, 6, 2, D), F32, kind="Internal").ap()
    build(nc, I, out, mod_dram)
    r = run_bass_kernel_spmd(nc, [{"in_" + k: v for k, v in arrays.items()}], core_ids=[0])
    return r.results[0]["out"].reshape(1, SEQ, D)
```

```python
import math
from contextlib import ExitStack

import numpy as np
import concourse.bass as bass
from concourse import mybir

F32 = mybir.dt.float32
U32 = mybir.dt.uint32
ALU = mybir.AluOpType
ACT = mybir.ActivationFunctionType
AX = mybir.AxisListType

P = 128
D = 1024
KB = D // P
SEQ, CTX = 512, 256
DEPTH = 2
GRID_W = 64
DH = 64
NA_HEADS, NA_KC, NA_KR = 8, 16, 8
QH, KVH = 16, 4
PH, NKEYS, TOPK = 8, 128, 16
HK = PH * TOPK
ALPHA = (2 * DEPTH) ** 0.25
EPS = 1e-6
NEG = -1e30
LOWEST = -3.0e38
CT, LT = CTX // P, SEQ // P
CTX_TILES, LAT_TILES = tuple(range(CT)), tuple(range(CT, CT + LT))
SHIFT1, SCALE1, GATE1, SHIFT2, SCALE2, GATE2 = range(6)
RPW = 2 * GRID_W - 1

WCH = KB * 512
WSLOT = WCH + 512
WRING = 2
GROUP = 8
GROUPS = HK // GROUP
DRING = 4
AHEAD = 2
LAST_SLOT = 127
W_ATTN, W_TOPK = 3, 4


def constants():
    t = {}
    t["ones"] = np.ones((1, P), np.float32)
    t["ident"] = np.eye(P, dtype=np.float32)
    a = 2 * np.pi * np.outer(np.arange(DH), np.arange(DH)) / DH
    fc = np.zeros((P, 2, P))
    for g in range(2):
        s = slice(g * DH, (g + 1) * DH)
        fc[s, 0, s], fc[s, 1, s] = np.cos(a), np.sin(a)
    t["chan_dft"] = fc.reshape(P, 2 * P).astype(np.float32)
    for name, n in (("lat", SEQ), ("ctx", CTX)):
        k = (np.outer(np.arange(n), np.arange(n)) % n) * 2 * np.pi / n
        s = 1 / math.sqrt(n * DH)
        cs = np.stack([np.cos(k) * s, -np.sin(k) * s]).reshape(2, n // P, P, n)
        t["tok_dft_" + name] = cs.transpose(2, 0, 1, 3).reshape(P, -1).astype(np.float32)
    col = np.arange(GRID_W)
    start = np.clip(col - NA_KC // 2, 0, GRID_W - NA_KC)
    ok = (col[None] >= start[:, None]) & (col[None] < start[:, None] + NA_KC)
    t["col_mask"] = np.tile(np.where(ok, 0, NEG), (2, 1)).astype(np.float32)
    q, k = np.arange(P)[:, None], np.arange(P)[None]
    band = np.zeros((P, 3, P))
    band[:, 0][k < q], band[:, 2][k > q] = NEG, NEG
    t["band_mask"] = band.reshape(P, 3 * P).astype(np.float32)
    rot = np.zeros((P, P))
    for m in range(P):
        if m % DH < DH // 2:
            rot[m + DH // 2, m] = -1
        else:
            rot[m - DH // 2, m] = 1
    t["rotate_half"] = rot.astype(np.float32)
    n_freq = DH // 4
    inv = (np.float32(10000.0) ** (-np.arange(n_freq, dtype=np.float32) / np.float32(n_freq))).astype(np.float32)
    tok = np.arange(SEQ)
    ang = np.concatenate([(tok // GRID_W).astype(np.float32)[:, None] * inv,
                          (tok % GRID_W).astype(np.float32)[:, None] * inv], -1)
    rope = np.stack([np.cos(ang), np.sin(ang)]).astype(np.float32)
    t["rope"] = np.tile(rope.transpose(2, 0, 1), (4, 1, 1)).reshape(P, 2 * SEQ).copy()
    t["iota16"] = np.tile(np.arange(TOPK, dtype=np.float32), (P, 1))
    return t


def is_lat(t):
    return t >= CT


def blocks_per_pair(T, blocks=4):
    return min(1024 // T, blocks)


def schedule():
    def attend(layer, t):
        heads = NA_HEADS if layer == 0 else QH
        return [(W_ATTN, ("attn", layer, t, k)) for k in range(heads + 2)]

    def out_proj(layer, t):
        return [(2, ("heads_out", layer, t)), (6, ("w_out", layer, t, 0)), (6, ("w_out", layer, t, 1)),
                (5, ("add_norm", layer, t))]

    def second_half(layer, t, w_topk=W_TOPK):
        jobs = [(4, ("mod2", layer, t)), (6, ("query", layer, t, 0)), (6, ("query", layer, t, 1))]
        for n in range(4):
            jobs += [(w_topk, ("topk", layer, t, h)) for h in (2 * n, 2 * n + 1)]
            if n + 2 < 4:
                jobs.append((6, ("query", layer, t, n + 2)))
        return jobs + [(1, ("topk_end", layer, t))]

    def ada(layer, *js):
        return [(6, ("ada", layer, j, h)) for j in js for h in range(2)]

    def mod1(layer, tiles):
        return [(4, ("mod1", layer, tiles, t)) for t in tiles]

    def project(layer, tiles, *ns):
        T, jobs = P * len(tiles), []
        for n in ns:
            if n < 3:
                per = blocks_per_pair(T)
                jobs += [(6 * per * T // 512, ("project", layer, tiles, n, b0)) for b0 in range(0, 4, per)]
            else:
                jobs += [(6 if layer else 12, ("project", layer, tiles, n, t0)) for t0 in range(0, len(tiles), 2)]
        return jobs

    def fourier(tiles):
        per = blocks_per_pair(P * len(tiles))
        return ([(2, ("fourier", tiles, "chan", i)) for i in range(len(tiles))]
                + [(3 * len(tiles), ("fourier", tiles, "tok", b0)) for b0 in range(0, 4, per)])

    def rope(tiles):
        return [(len(tiles), ("rope", tiles, n)) for n in range(3)]

    def spread(jobs):
        slots, total, at = [[] for _ in range(HK)], sum(w for w, _ in jobs), 0
        for w, job in jobs:
            slots[int((at + w / 2) * LAST_SLOT / total)].append(job)
            at += w
        return slots

    def beside(steps, jobs):
        assert len(jobs) <= len(steps) - 1
        mixed = steps[:1]
        for n, item in enumerate(steps[1:]):
            mixed += [item] + jobs[n:n + 1]
        return mixed

    lat, ctx = LAT_TILES, CTX_TILES
    g1, sh2, sc2 = ada(0, GATE1), ada(0, SHIFT2), ada(0, SCALE2)
    k_lat = project(0, lat, 2)
    att, outp, half, m1 = attend(0, 0), out_proj(0, 0), second_half(0, 0), mod1(0, lat)
    start = (ada(0, SHIFT1, SCALE1) + g1 + mod1(0, ctx) + project(0, ctx, 0) + m1[:1] + fourier(ctx) + m1[1:2]
             + beside(project(0, ctx, 1, 2, 3), m1[2:]) + beside(att, sh2) + outp + sc2
             + half[:6] + k_lat[:1] + half[6:9] + k_lat[1:] + half[9:])
    h1, p0, fo = second_half(0, 1, 6), project(0, lat, 0), fourier(lat)
    background = {
        (0, 0): attend(0, 1) + out_proj(0, 1) + h1[:9] + p0[:1] + h1[9:10] + p0[1:] + h1[10:11] + fo[:2]
        + h1[11:12] + fo[2:5] + h1[12:] + fo[5:] + project(0, lat, 1, 3),
        (0, 1): beside(attend(0, 2), ada(0, GATE2) + ada(1, 0, 1)) + out_proj(0, 2) + second_half(0, 2),
        (0, 2): beside(attend(0, 3), ada(1, 2, 3)) + out_proj(0, 3) + second_half(0, 3),
        (0, 3): beside(attend(0, 4), ada(1, 4, 5)) + out_proj(0, 4) + second_half(0, 4),
        (0, 4): attend(0, 5) + out_proj(0, 5) + mod1(1, ctx) + project(1, ctx, 2, 3) + second_half(0, 5),
        (0, 5): mod1(1, lat[0:2]) + project(1, lat[0:2], 0, 1, 2, 3)
        + rope(lat[0:2]) + attend(1, 2) + out_proj(1, 2) + second_half(1, 2),
        (1, 2): mod1(1, lat[2:3]) + project(1, lat[2:3], 0, 1, 2, 3) + rope(lat[2:3])
        + attend(1, 3) + out_proj(1, 3) + second_half(1, 3),
        (1, 3): mod1(1, lat[3:4]) + project(1, lat[3:4], 0, 1, 2, 3) + rope(lat[3:4])
        + attend(1, 4) + out_proj(1, 4) + second_half(1, 4),
        (1, 4): attend(1, 5) + out_proj(1, 5) + second_half(1, 5),
    }
    order = [(0, t) for t in ctx + lat] + [(1, t) for t in lat]
    phases = [(a, b, spread(background[a]) if a in background else None)
              for a, b in zip(order + [None], [None] + order)]
    return [job for _, job in start], phases, order


def build(nc, I, out, mod_dram):
    es = ExitStack()
    with es:
        def sb(name, cols, dt=F32):
            return es.enter_context(nc.sbuf_tensor(name, [P, cols], dt))

        def sem(name):
            return es.enter_context(nc.semaphore(name))

        def view(ap, k):
            return ap.rearrange("p (k n) -> p k n", k=k)

        start_jobs, phases, tile_order = schedule()
        tile_no = {lt: n for n, lt in enumerate(tile_order)}

        x_state = sb("x_state", (CT + LT) * D)
        wring = sb("wring", WRING * WSLOT)
        u_ring = sb("u_rows", GROUP * D)
        u_rows = view(u_ring, GROUP)
        v_ring = sb("v_rows", GROUP * D)
        v_rows = view(v_ring, GROUP)
        kv = sb("kv", 10240)
        h_tok = view(sb("h_tok", 2 * D), 2)
        scores_sb = view(sb("scores_sb", 1024), 2)
        work = sb("work", D)
        otok = sb("otok", D)
        probs_sb = sb("probs_sb", 2 * 768)
        probs_t = sb("probs_t", 768)
        bias_sb = sb("bias_sb", 1024)
        diags = view(sb("diags", DRING * P), DRING)
        ident = sb("ident", P)
        col_mask = sb("col_mask", GRID_W)
        band_mask = sb("band_mask", 3 * P)
        rot = sb("rot", P)
        iota16 = sb("iota16", TOPK)
        sinks, sinks_exp = sb("sinks", QH), sb("sinks_exp", QH)
        silu_c = sb("silu_c", KB * 2)
        bnst, mv = sb("bnst", 12), sb("mv", 2)
        ve, sd, rs, rt = sb("ve", 1), sb("sd", 1), sb("rs", 1), sb("rt", 1)
        negm, den, rden = sb("negm", QH), sb("den", QH), sb("rden", QH)
        acts = sb("acts", HK)
        cc, cc_exp = acts[:, 0:KB * 2], acts[:, KB * 2:KB * 4]
        ones = sb("ones", P)
        gates = [sb(f"gates{i}", HK) for i in range(2)]
        idx_tok = [sb(f"idx_tok{i}", HK, U32) for i in range(3)]
        wts = [sb(f"wts{i}", HK) for i in range(2)]
        stage_u = sb("stage_u", 2 * GROUP, U32)
        stage_v = sb("stage_v", 2 * GROUP, U32)
        tiu = sb("tiu", 2 * TOPK, U32)
        bv, bpu = sb("bv", HK), sb("bpu", TOPK, U32)
        bij_u = sb("bij_u", 2 * TOPK, U32)
        tv, tif, bij, e12 = (probs_sb[:, 768 + i * 2 * TOPK:768 + (i + 1) * 2 * TOPK] for i in range(4))
        idx_f, gsum = probs_sb[:, 896:896 + TOPK], probs_sb[:, 912:912 + PH]

        def X(t):
            return x_state[:, t * D:(t + 1) * D]

        k_lat, v_lat = view(kv[:, 0:2048], 4), view(kv[:, 2048:4096], 4)
        q_lat, fy_lat = view(kv[:, 4096:6144], 4), view(kv[:, 8192:10240], 4)
        k_ctx, v_ctx = view(kv[:, 6144:7168], 4), view(kv[:, 7168:8192], 2)
        q_ctx, fy_ctx = view(kv[:, 4096:5120], 4), view(kv[:, 8192:9216], 4)
        q1, k1, v1 = view(kv[:, 0:2048], 8), view(kv[:, 2048:4096], 4), view(kv[:, 4096:5120], 4)
        k1_ctx, v1_ctx = view(kv[:, 5120:6144], 4), view(kv[:, 6144:6656], 2)
        at1 = kv[:, 6656:8704]
        rope_sb = view(kv[:, 8704:9728], 2)
        at0 = v_ring[:, 0:4096]
        pq = view(v_ring[:, 4096:8192], 4)
        peer_t = view(otok[:], KB)
        heads_t = view(work[:], KB)
        probs = view(probs_sb[:], 2)
        queries_t = view(probs_sb[:, 0:512], 4)
        cand, onehot, rest = probs_t[:, 0:256], probs_t[:, 256:512], probs_t[:, 512:768]
        bias = view(bias_sb[:], 2)
        chan_dft = bias_sb[:, 0:2 * P]
        mod_row = work[0:2, :]

        def modulated_t(layer, T):
            if layer == 0 and T == CTX:
                return view(v_ring[:, 6144:8192], KB)
            return view((at0 if layer == 0 else at1)[:, 0:KB * T], KB)

        def projected(layer, tiles, n):
            T, lat = P * len(tiles), is_lat(tiles[0])
            scale = DH ** -0.5
            if layer == 0:
                return [(q_lat if lat else q_ctx, 1.0), (q_lat if lat else q_ctx, scale),
                        (k_lat if lat else k_ctx, 1.0), (v_lat if lat else v_ctx, 1.0)][n]
            if not lat:
                return {2: (k1_ctx, 1.0), 3: (v1_ctx, 1.0)}[n]
            i = tiles[0] - CT
            c = (i % 2) * P
            return [(q1[:, 0:4, c:c + T], scale), (q1[:, 4:8, c:c + T], scale),
                    (k1[:, :, i * P:i * P + T], 1.0), (v1[:, i:i + len(tiles), :], 1.0)][n]

        def unit(layer, t, h):
            p = slice(64 * (h % 2), 64 * (h % 2) + 64)
            i = t - CT if is_lat(t) else t
            if layer == 0:
                c = slice(h * DH, (h + 1) * DH)
                vals = [v_ctx[:, m, c] for m in range(CT)]
                kc = k_ctx[p, h // 2, 0:CTX]
                if not is_lat(t):
                    return q_ctx[p, h // 2, i * P:(i + 1) * P], None, 512, kc, vals
                return (q_lat[p, h // 2, i * P:(i + 1) * P], k_lat[p, h // 2, :], 0, kc,
                        [v_lat[:, m, c] for m in range(LT)] + vals)
            g = h // (QH // KVH)
            c = slice(g * DH, (g + 1) * DH)
            t0, t1 = max(i - 1, 0), min(i + 1, LT - 1)
            q0 = (i % 2) * P
            return (q1[p, h // 2, q0:q0 + P], k1[p, g, t0 * P:(t1 + 1) * P], 512 - (t1 - t0 + 1) * P,
                    k1_ctx[p, g, 0:CTX], [v1[:, m, c] for m in range(t0, t1 + 1)] + [v1_ctx[:, m, c] for m in range(CT)])

        pairs = [es.enter_context(nc.psum_tensor(f"pair{i}", [P, 1024], F32)) for i in range(3)]
        facc = es.enter_context(nc.psum_tensor("facc", [P, 1024], F32))

        const_in, c_in = sem("const_in"), sem("c_in")
        ctx_in, latents_in = sem("ctx_in"), sem("latents_in")
        mod_out, mod_row_ready = sem("mod_out"), sem("mod_row_ready")
        cc_exp_done, silu_done = sem("cc_exp_done"), sem("silu_done")
        chunk_in = [sem(f"chunk_in{i}") for i in range(WRING + 1)]
        pair_full = [sem(f"pair_full{i}") for i in range(3)]
        pair_free = [sem(f"pair_free{i}") for i in range(3)]
        dve_step = sem("dve_step")
        ln_var, ln_sd = sem("ln_var"), sem("ln_sd")
        work_free = sem("work_free")
        normed = sem("normed")
        h_ready = sem("h_ready")
        rope_in, roped = sem("rope_in"), sem("roped")
        bias_in, bias_free = [sem(f"bias_in{i}") for i in range(2)], sem("bias_free")
        negm_ready, exp_done, pt_ready, pv_done = sem("negm_ready"), sem("exp_done"), sem("pt_ready"), sem("pv_done")
        half_out = sem("half_out")
        sink_sub, sink_exp = sem("sink_sub"), sem("sink_exp")
        o_ready = sem("o_ready")
        x_done = sem("x_done")
        scores_free = sem("scores_free")
        gate_sub, gate_exp = sem("gate_sub"), sem("gate_exp")
        idx_ready = sem("idx_ready")
        u_in = [sem(f"u_in{i}") for i in range(GROUP)]
        v_in = [sem(f"v_in{i}") for i in range(GROUP)]
        u_used, v_used = sem("u_used"), sem("v_used")
        staged = sem("staged")
        acts_ready, gelu_done, wts_ready = sem("acts_ready"), sem("gelu_done"), sem("wts_ready")
        diag_ready, f_free = sem("diag_ready"), sem("f_free")
        out_done = sem("out_done")

        taken = {}

        def take(name, eng, s, n=1):
            taken[name, s.name] = taken.get((name, s.name), 0) + n
            eng.wait_ge(s, taken[name, s.name])

        all_jobs = start_jobs + [j for _, _, slots in phases if slots for jobs in slots for j in jobs]
        rope_jobs = [job for job in all_jobs if job[0] == "rope"]

        chunks, chunk_no, chunk_freed = [], {}, {}

        def chunk(name, *srcs):
            chunk_no[name] = len(chunks)
            chunks.append((name, srcs))

        def modvec(layer, t, j):
            row = 0 if is_lat(t) else 1
            return bass.AP(mod_dram.tensor, ((layer * 6 + j) * 2 + row) * D, [[0, 1], [1, D]])

        def postvec(which, layer, j):
            return bass.AP(I[which].tensor, (layer * 2 + j) * D, [[0, 1], [1, D]])

        def chunks_of(job):
            kind, layer = job[0], job[1]
            if kind == "ada":
                n = 2 * job[2] + job[3]
                src = bass.AP(I["ada_b"].tensor, layer * 6 * D + n * 512, [[0, 2], [1, 512]])
                chunk(job, (I["ada_w"][layer, n], 0, P), (src, WCH, 2))
            elif kind == "mod1":
                chunk(job, (modvec(layer, job[3], SCALE1), 0, 1), (modvec(layer, job[3], SHIFT1), D, 1))
            elif kind == "project" and job[4] == 0:
                n = job[3]
                w = I["even_w_in"][n] if layer == 0 else I["odd_w_v"] if n == 3 else I["odd_w_in"][n]
                chunk(job[:4], (w, 0, P))
            elif kind == "fourier" and job[2:] == ("chan", 0):
                chunk(job[:2], (I["tok_dft_lat" if is_lat(job[1][0]) else "tok_dft_ctx"], 0, P))
            elif kind == "w_out":
                chunk(job, (I["even_w_out" if layer == 0 else "odd_w_out"][job[3]], 0, P))
            elif kind == "add_norm":
                chunk(job, (modvec(layer, job[2], GATE1), 0, 1), (postvec("post_g", layer, 0), D, 1),
                      (postvec("post_b", layer, 0), 2 * D, 1))
            elif kind == "mod2":
                chunk(job, (modvec(layer, job[2], SCALE2), 0, 1), (modvec(layer, job[2], SHIFT2), D, 1))
            elif kind == "query":
                chunk(job, (I["peer_w_q"][layer, job[3]], 0, P))
            elif kind == "close":
                chunk(job, (modvec(layer, job[2], GATE2), 0, 1), (postvec("post_g", layer, 1), D, 1),
                      (postvec("post_b", layer, 1), 2 * D, 1))

        in_order = list(start_jobs)
        for _, v_tile, slots in phases:
            in_order += [job for jobs in slots or [] for job in jobs]
            if v_tile is not None:
                in_order.append(("close",) + v_tile)
        chunks_by = []
        for job in in_order:
            chunks_of(job)
            chunks_by.append(len(chunks))
        early = chunk_no["mod2", 0, 0]
        chunk_slot = [n % 3 if n < early else (n - early) % 2 for n in range(len(chunks))]
        slot_ap = [wring[:, 0:WSLOT], wring[:, WSLOT:2 * WSLOT], u_ring[:, 0:WSLOT]]
        chunk_need, before, seen, last_in = [], [], [0] * 3, [-1] * 3
        for n, (_, srcs) in enumerate(chunks):
            i = chunk_slot[n]
            seen[i] += 16 * len(srcs)
            chunk_need.append(seen[i])
            before.append(last_in[i])
            last_in[i] = n

        def slot(eng, name):
            n = chunk_no[name]
            eng.wait_ge(chunk_in[chunk_slot[n]], chunk_need[n])
            return slot_ap[chunk_slot[n]]

        claimed, claims = {}, [0]

        def claim(pe, name):
            i, n = claims[0] % 3, claims[0] // 3
            claims[0] += 1
            claimed[name] = (i, n)
            if n:
                pe.wait_ge(pair_free[i], n)
            return pairs[i], pair_full[i]

        def filled(eng, name):
            i, n = claimed[name]
            eng.wait_ge(pair_full[i], n + 1)
            return pairs[i], pair_free[i], n + 1

        def emptied(eng, name):
            i, n = claimed[name]
            eng.wait_ge(pair_free[i], n + 1)

        block = es.enter_context(nc.Block())

        @block.tensor
        def _(pe):
            def mm(o, lhsT, rhs, start, stop):
                return nc.tensor.matmul(o, lhsT=lhsT, rhs=rhs, start=start, stop=stop, skip_group_check=True)

            def last_use(name):
                chunk_freed[name] = pair_full[(claims[0] - 1) % 3], (claims[0] - 1) // 3 + 1

            def weights(name, cols=512):
                return view(slot(pe, name)[:, 0:KB * cols], KB)

            def vectors(job, count):
                sl = slot(pe, job)
                for j in range(count):
                    pair, full = claim(pe, job + ("vec", j))
                    for c in range(2):
                        last = mm(pair[:, c * 512:(c + 1) * 512], ones[0:1, :],
                                  sl[0:1, j * D + c * 512:j * D + (c + 1) * 512], True, True)
                    last.then_inc(full, 1)
                last_use(job)

            def transposes(name, src, blocks):
                pair, full = claim(pe, name)
                for k in range(blocks):
                    last = nc.tensor.transpose(pair[:, k * P:(k + 1) * P], src[:, k * P:(k + 1) * P], ident[:])
                last.then_inc(full, 1)

            def ada(job):
                sc = silu_c[:].rearrange("p (k c) -> p k c", k=KB)
                pair, full = claim(pe, job)
                w = weights(job)
                for k in range(KB):
                    last = mm(pair[0:2, 0:512], sc[:, k, :], w[:, k, :], k == 0, k == KB - 1)
                i, n = claimed[job]
                chunk_freed[job] = pair_free[i], n + 1
                last.then_inc(full, 1)

            def mod1(job):
                vectors(job, 2)
                take("pe", pe, h_ready)
                transposes(job, work[:], KB)

            def project(job):
                _, layer, tiles, n, first = job
                T = P * len(tiles)
                for t in tiles:
                    emptied(pe, ("mod1", layer, tiles, t))
                src = modulated_t(layer, T)
                pair, full = claim(pe, job)
                if n < 3:
                    w = weights(job[:4])
                    for j in range(blocks_per_pair(T)):
                        for k in range(KB):
                            last = mm(pair[:, j * T:(j + 1) * T], w[:, k, (first + j) * P:(first + j + 1) * P],
                                      src[:, k, :], k == 0, k == KB - 1)
                else:
                    width = 512 if layer == 0 else KVH * DH
                    w = weights(job[:4], width)
                    for j in range(min(2, len(tiles))):
                        for k in range(KB):
                            last = mm(pair[:, j * 512:j * 512 + width], src[:, k, (first + j) * P:(first + j + 1) * P],
                                      w[:, k, :], k == 0, k == KB - 1)
                last.then_inc(full, 1)
                last_use(job[:4])

            def fourier(job):
                _, tiles, stage, first = job
                nt, T = len(tiles), P * len(tiles)
                ft = projected(0, tiles, 0)[0]
                if job[2:] == ("chan", 0):
                    for b0 in range(0, 4, blocks_per_pair(T)):
                        emptied(pe, ("project", 0, tiles, 0, b0))
                if job[2:] == ("tok", 0):
                    for i in range(nt):
                        emptied(pe, ("fourier", tiles, "chan", i))
                pair, full = claim(pe, job)
                if stage == "chan":
                    for b in range(4):
                        last = mm(pair[:, b * 256:(b + 1) * 256], ft[:, b, first * P:(first + 1) * P], chan_dft,
                                  True, True)
                else:
                    w = view(slot(pe, job[:2])[:, 0:2 * nt * T], 2 * nt)
                    for j in range(blocks_per_pair(T)):
                        for k in range(2 * nt):
                            c = (first + j) * 256 + (k // nt) * P
                            last = mm(pair[:, j * T:(j + 1) * T], pq[:, k % nt, c:c + P], w[:, k, :],
                                      k == 0, k == 2 * nt - 1)
                    last_use(job[:2])
                last.then_inc(full, 1)

            def rope(job):
                _, tiles, n = job
                T = P * len(tiles)
                dst, _ = projected(1, tiles, n)
                for b0 in range(0, 4, blocks_per_pair(T)):
                    emptied(pe, ("project", 1, tiles, n, b0))
                pair, full = claim(pe, job)
                for b in range(4):
                    last = mm(pair[:, b * T:(b + 1) * T], rot[:], dst[:, b, :], True, True)
                last.then_inc(full, 1)

            def attn(job):
                _, layer, t, k = job
                if k == 0 and layer == 0:
                    tiles = LAT_TILES if is_lat(t) else CTX_TILES
                    for n in (1, 2):
                        for b0 in range(0, 4, blocks_per_pair(P * len(tiles))):
                            emptied(pe, ("project", 0, tiles, n, b0))
                    for t0 in range(0, len(tiles), 2):
                        emptied(pe, ("project", 0, tiles, 3, t0))
                if k == 0 and layer == 1:
                    for tiles in (CTX_TILES, LAT_TILES[0:2], LAT_TILES[2:3], LAT_TILES[3:4]):
                        if ("project", 1, tiles, 3, 0) in claimed:
                            emptied(pe, ("project", 1, tiles, 3, 0))
                        if ("rope", tiles, 2) in claimed:
                            pe.wait_ge(roped, rope_jobs.index(("rope", tiles, 2)) + 1)
                    emptied(pe, ("project", 1, CTX_TILES, 2, 0))
                heads = NA_HEADS if layer == 0 else QH
                if k >= 2:
                    _, _, lo, _, vals = unit(layer, t, k - 2)
                    i, _ = claimed["t", layer, t, k - 2]
                    take("pe", pe, pt_ready)
                    for n, b in enumerate(range(lo // P, 6)):
                        last = mm(pairs[i][:, 768:768 + DH], probs_t[:, b * P:(b + 1) * P], vals[n], n == 0, b == 5)
                    last.then_inc(pv_done, 1)
                if 1 <= k <= heads:
                    h = k - 1
                    lo = unit(layer, t, h)[2]
                    take("pe", pe, exp_done)
                    pair, full = claim(pe, ("t", layer, t, h))
                    for b in range(lo // P, 6):
                        last = nc.tensor.transpose(pair[:, b * P:(b + 1) * P], probs[:, h % 2, b * P:(b + 1) * P], ident[:])
                    last.then_inc(full, 1)
                if k < heads:
                    q, kl, lo, kc, _ = unit(layer, t, k)
                    pair, full = claim(pe, ("s", layer, t, k))
                    if kl is not None:
                        mm(pair[:, lo:512], q, kl, True, True)
                    mm(pair[:, 512:768], q, kc, True, True).then_inc(full, 1)

            def heads_out(job):
                take("pe", pe, o_ready)
                transposes(job, otok[:], 4 if job[1] == 0 else 8)

            half_outs = [0]

            def w_out(job):
                _, layer, t, n = job
                lat = is_lat(t)
                i = t - CT if lat else t
                emptied(pe, ("heads_out", layer, t))
                if layer == 0 and i == 0:
                    for b0 in range(0, 4, 2 if lat else 4):
                        emptied(pe, ("fourier", LAT_TILES if lat else CTX_TILES, "tok", b0))
                fy = fy_lat if lat else fy_ctx
                if layer == 0:
                    blocks = [fy[:, b, i * P:(i + 1) * P] for b in range(4)] + [heads_t[:, b, :] for b in range(4)]
                else:
                    blocks = [heads_t[:, b, :] for b in range(8)]
                if n == 0:
                    claim(pe, job[:3])
                j, c = claimed[job[:3]]
                w = weights(job)
                for k in range(KB):
                    last = mm(pairs[j][:, n * 512:(n + 1) * 512], blocks[k], w[:, k, :], k == 0, k == KB - 1)
                if n == 0:
                    half_outs[0] += 1
                    chunk_freed[job] = half_out, half_outs[0]
                    last.then_inc(half_out, 1)
                else:
                    chunk_freed[job] = pair_full[j], c + 1
                    last.then_inc(pair_full[j], 1)

            def mod2(job):
                _, layer, t = job
                vectors(job, 2)
                take("pe", pe, h_ready)
                transposes(job, h_tok[:, tile_no[layer, t] % 2, :], KB)

            def query(job):
                _, layer, t, n = job
                if n == 0:
                    emptied(pe, ("mod2", layer, t))
                sl = slot(pe, job)
                w = view(sl[:, 0:WCH], KB)
                pair, full = claim(pe, job)
                for b in range(4):
                    for k in range(KB):
                        last = mm(pair[:, b * P:(b + 1) * P], w[:, k, b * P:(b + 1) * P], peer_t[:, k, :],
                                  k == 0, k == KB - 1)
                last.then_inc(full, 1)
                emptied(pe, job)
                pair, full = claim(pe, job + ("scores",))
                for b in range(4):
                    last = mm(pair[:, b * P:(b + 1) * P], queries_t[:, b, :], sl[:, WCH + b * P:WCH + (b + 1) * P],
                              True, True)
                last.then_inc(full, 1)
                last_use(job)

            do = dict(ada=ada, mod1=mod1, project=project, fourier=fourier, rope=rope, attn=attn,
                      heads_out=heads_out, w_out=w_out, add_norm=lambda job: vectors(job, 3), mod2=mod2, query=query)

            def accumulate(group, g, r, start):
                pe.wait_ge(v_in[r], g * 16 + 16 * (group + 1))
                pe.wait_ge(diag_ready, g * GROUP + (group * GROUP + r + 1))
                for c in range(2):
                    last = mm(facc[:, c * 512:(c + 1) * 512], diags[:, r % DRING, :],
                              v_rows[:, r, c * 512:(c + 1) * 512], start, False)
                last.then_inc(v_used, 1)

            take("pe", pe, silu_done)
            for job in start_jobs:
                if job == ("mod1", 0, CTX_TILES, 0):
                    pe.wait_ge(const_in, 16 * 8)
                if job[0] in do:
                    do[job[0]](job)
            for _, v_tile, slots in phases:
                first = tile_no[v_tile] * GROUPS if v_tile is not None else 0
                if v_tile is not None and tile_no[v_tile]:
                    pe.wait_ge(f_free, tile_no[v_tile])
                if slots is None:
                    if v_tile is not None:
                        for r in range(GROUP):
                            accumulate(first, 0, r, r == 0)
                        with pe.Fori(1, GROUPS) as g:
                            for r in range(GROUP):
                                accumulate(first, g, r, False)
                for s, jobs in enumerate(slots or []):
                    if v_tile is not None:
                        accumulate(first + s // GROUP, 0, s % GROUP, s == 0)
                    for job in jobs:
                        if job[0] in do:
                            do[job[0]](job)
                if v_tile is not None:
                    vectors(("close",) + v_tile, 3)

        @block.scalar
        def _(act):
            def evac(name, dst, src, scale=1.0):
                pair, free, n = filled(act, name)
                nc.scalar.activation(dst, src(pair), ACT.Copy, scale=scale).then_inc(free, 1)

            def gate_to_work(job):
                take("act", act, work_free)
                evac(job + ("vec", 0), work[:], lambda pair: pair[:])

            def add_norm(job):
                gate_to_work(job)
                sqrt_of_variance()

            def sqrt_of_variance():
                take("act", act, ln_var)
                nc.scalar.activation(sd[:], ve[:], ACT.Sqrt).then_inc(ln_sd, 1)

            def mod1(job):
                _, layer, tiles, t = job
                at, i = modulated_t(layer, P * len(tiles)), tiles.index(t)
                sqrt_of_variance()
                evac(job, at[:, :, i * P:(i + 1) * P], lambda pair: view(pair[:], KB))

            def project(job):
                _, layer, tiles, n, first = job
                T = P * len(tiles)
                dst, scale = projected(layer, tiles, n)
                if n < 3:
                    per = blocks_per_pair(T)
                    evac(job, dst[:, first:first + per, :], lambda pair: view(pair[:, 0:per * T], per), scale)
                else:
                    width, per = (512 if layer == 0 else KVH * DH), min(2, len(tiles))
                    evac(job, dst[:, first:first + per, :], lambda pair: view(pair[:], 2)[:, 0:per, 0:width])

            def fourier(job):
                _, tiles, stage, first = job
                if stage == "chan":
                    evac(job, pq[:, first, :], lambda pair: pair[:])
                else:
                    fy, per = (fy_lat if is_lat(tiles[0]) else fy_ctx), blocks_per_pair(P * len(tiles))
                    evac(job, fy[:, first:first + per, :], lambda pair: view(pair[:], per))

            units_done = [0]

            def attn(job):
                _, layer, t, k = job
                heads = NA_HEADS if layer == 0 else QH
                lo = unit(layer, t, 0)[2]
                if 1 <= k <= heads:
                    i, n = claimed["t", layer, t, k - 1]
                    act.wait_ge(pair_full[i], n + 1)
                    if units_done[0]:
                        act.wait_ge(pv_done, units_done[0])
                    units_done[0] += 1
                    nc.scalar.activation(probs_t[:, lo:768], pairs[i][:, lo:768], ACT.Copy).then_inc(pt_ready, 1)
                if k < heads:
                    take("act", act, negm_ready)
                    i, n = claimed["s", layer, t, k]
                    nc.scalar.activation(probs[:, k % 2, lo:768], pairs[i][:, lo:768], ACT.Exp,
                                         bias=negm[:, k:k + 1], accum_out=den[:, k:k + 1]).then_inc(pair_free[i], 1)
                    act.wait_ge(pair_free[i], n + 1)
                    nc.scalar.sem_inc(exp_done, 1)

            def heads_out(job):
                blocks = 4 if job[1] == 0 else 8
                if job[1] == 1:
                    take("act", act, sink_sub)
                    nc.scalar.activation(sinks_exp[:], sinks_exp[:], ACT.Exp).then_inc(sink_exp, 1)
                evac(job, heads_t[:, 0:blocks, :], lambda pair: view(pair[:, 0:blocks * P], blocks))

            def mod2(job):
                sqrt_of_variance()
                evac(job, peer_t, lambda pair: view(pair[:], KB))

            queries_done = [0]

            def query(job):
                n = job[3]
                evac(job, queries_t, lambda pair: view(pair[:, 0:512], 4))
                if queries_done[0] >= 2:
                    act.wait_ge(scores_free, queries_done[0] - 1)
                queries_done[0] += 1
                evac(job + ("scores",), scores_sb[:, n % 2, :], lambda pair: pair[:, 0:512])

            def topk_end(job):
                b = tile_no[job[1:]] % 2
                take("act", act, gate_sub)
                nc.scalar.activation(gates[b][:], gates[b][:], ACT.Exp).then_inc(gate_exp, 1)

            do = dict(mod1=mod1, project=project, fourier=fourier, attn=attn, heads_out=heads_out,
                      add_norm=add_norm, mod2=mod2, query=query, topk_end=topk_end)

            def diagonal(b, first, s, g=None):
                need = first + s + 1 - DRING + GROUP
                act.wait_ge(v_used, need if g is None else g * GROUP + need)
                scale = wts[b][:, s:s + 1] if g is None else wts[b][:, bass.ds(g * GROUP + s, 1)]
                nc.scalar.activation(diags[:, s % DRING, :], ident[:], ACT.Copy, scale=scale).then_inc(diag_ready, 1)

            act.wait_ge(c_in, 16)
            nc.scalar.activation(cc_exp, cc, ACT.Exp, scale=-1.0).then_inc(cc_exp_done, 1)
            for job in start_jobs:
                if job[0] in do:
                    do[job[0]](job)
            for u_tile, v_tile, slots in phases:
                if v_tile is not None:
                    n = tile_no[v_tile]
                    first = n * HK
                    act.wait_ge(wts_ready, n + 1)
                if slots is None:
                    if v_tile is not None:
                        with act.Fori(0, GROUPS) as g:
                            for r in range(GROUP):
                                diagonal(n % 2, first, r, g)
                else:
                    if v_tile is not None:
                        for s in range(AHEAD):
                            diagonal(n % 2, first, s)
                    for s, jobs in enumerate(slots):
                        if v_tile is not None and s + AHEAD < HK:
                            diagonal(n % 2, first, s + AHEAD)
                        for job in jobs:
                            if job[0] in do:
                                do[job[0]](job)
                if u_tile is not None:
                    take("act", act, acts_ready)
                    nc.scalar.activation(acts[:], acts[:], ACT.Gelu).then_inc(gelu_done, 1)
                if v_tile is not None:
                    add_norm(("close",) + v_tile)

        @block.vector
        def _(v):
            V = nc.vector
            counts = {}

            def signal(ins, s):
                counts[s.name] = counts.get(s.name, 0) + 1
                ins.then_inc(s, 1)
                v.wait_ge(s, counts[s.name])

            def step(ins):
                signal(ins, dve_step)

            def last_read(ins, free, count):
                ins.then_inc(free, 1)
                v.wait_ge(free, count)

            def statistics(t):
                for h in range(2):
                    step(V.bn_stats(bnst[:, 6 * h:6 * h + 6], X(t)[:, h * 512:(h + 1) * 512]))
                step(V.bn_aggr(mv[:], bnst[:]))
                signal(V.tensor_scalar(ve[:], mv[:, 1:2], EPS, None, ALU.add), ln_var)
                take("dve", v, ln_sd)
                step(V.reciprocal(rs[:], sd[:]))
                step(V.tensor_tensor(rt[:], rs[:], rs[:], ALU.mult))
                step(V.tensor_tensor(rt[:], rt[:], ve[:], ALU.mult))
                step(V.tensor_scalar(rt[:], rt[:], -0.5, 1.5, ALU.mult, ALU.add))
                step(V.tensor_tensor(rs[:], rs[:], rt[:], ALU.mult))

            def vector(job, j):
                pair, fr, n = filled(v, job + ("vec", j))
                return pair[:], fr, n

            def normalised(job, t, dst, first, done):
                scale, fr, n = vector(job, first)
                last_read(V.scalar_tensor_tensor(dst, X(t), mv[:, 0:1], scale, ALU.subtract, ALU.mult), fr, n)
                shift, fr, n = vector(job, first + 1)
                last_read(V.scalar_tensor_tensor(dst, dst, rs[:], shift, ALU.mult, ALU.add), fr, n)
                V.sem_inc(done, 1)

            rows_made = [0]

            def row_stored():
                if rows_made[0]:
                    v.wait_ge(mod_out, 16 * rows_made[0])

            def ada(job):
                _, layer, j, h = job
                pair, fr, n = filled(v, job)
                if h == 0:
                    row_stored()
                rows_made[0] += h
                one = 1.0 if j in (SCALE1, SCALE2) else 0.0
                sl = slot(v, job)
                last_read(V.scalar_tensor_tensor(mod_row[:, h * 512:(h + 1) * 512], pair[0:2, 0:512], one,
                                                 sl[0:2, WCH:WCH + 512], ALU.add, ALU.add), fr, n)
                if h:
                    V.sem_inc(mod_row_ready, 1)

            def mod1(job):
                _, layer, tiles, t = job
                i = tiles.index(t)
                statistics(t)
                if i:
                    filled(v, job[:3] + (tiles[i - 1],))
                row_stored()
                normalised(job, t, work[:], 0, h_ready)

            def rope(job):
                _, tiles, n = job
                T, i = P * len(tiles), tiles[0] - CT
                v.wait_ge(rope_in, 16)
                wide = [P, 4, T]
                cos, sin = (rope_sb[:, m, i * P:i * P + T].unsqueeze(1).to_broadcast(wide) for m in range(2))
                a, b = view(work[:, 0:4 * T], 4), view(otok[:, 0:4 * T], 4)
                dst, _ = projected(1, tiles, n)
                pair, fr, cnt = filled(v, job)
                last_read(V.tensor_tensor(a, view(pair[:, 0:4 * T], 4), sin, ALU.mult), fr, cnt)
                step(V.tensor_tensor(b, dst, cos, ALU.mult))
                signal(V.tensor_tensor(dst, a, b, ALU.add), roped)

            biases = [0]

            def attn(job):
                _, layer, t, k = job
                i = t - CT
                if k >= 2:
                    take("dve", v, pv_done)
                    j, n = claimed["t", layer, t, k - 2]
                    last_read(V.tensor_copy(otok[:, (k - 2) * DH:(k - 1) * DH], pairs[j][:, 768:768 + DH]),
                              pair_free[j], n + 1)
                if k < (NA_HEADS if layer == 0 else QH):
                    lo = unit(layer, t, k)[2]
                    pair, _, _ = filled(v, ("s", layer, t, k))
                    local, negm_k = pair[:, lo:512], negm[:, k:k + 1]
                    if layer == 0 and is_lat(t):
                        b = biases[0] % 2
                        v.wait_ge(bias_in[b], 32 * (biases[0] // 2 + 1))
                        biases[0] += 1
                        signal(V.tensor_tensor(local, local, bias[:, b, :], ALU.add), bias_free)
                        wide = [P, NA_KR, GRID_W]
                        step(V.tensor_tensor(view(local, NA_KR), view(local, NA_KR),
                                             col_mask[:].unsqueeze(1).to_broadcast(wide), ALU.add))
                    if layer == 1:
                        m0 = (max(i - 1, 0) - i + 1) * P
                        step(V.tensor_tensor(local, local, band_mask[:, m0:m0 + 512 - lo], ALU.add))
                        step(V.tensor_reduce(negm_k, pair[:, lo:768], AX.X, ALU.max))
                        signal(V.tensor_scalar(negm_k, negm_k, sinks[:, k:k + 1], -1.0, ALU.max, ALU.mult), negm_ready)
                    else:
                        signal(V.tensor_reduce(negm_k, pair[:, lo:768], AX.X, ALU.max, negate=True), negm_ready)

            def heads_out(job):
                heads = NA_HEADS if job[1] == 0 else QH
                r = slice(0, heads)
                if job[1] == 1:
                    signal(V.tensor_tensor(sinks_exp[:], sinks[:], negm[:], ALU.add), sink_sub)
                    take("dve", v, sink_exp)
                    step(V.tensor_tensor(den[:], den[:], sinks_exp[:], ALU.add))
                row_stored()
                step(V.reciprocal(rden[:, r], den[:, r]))
                o = view(otok[:, 0:heads * DH], heads)
                signal(V.tensor_tensor(o, o, rden[:, r].unsqueeze(2).to_broadcast([P, heads, DH]), ALU.mult), o_ready)

            def add_norm(job):
                _, layer, t = job
                pair, fr, n = filled(v, ("w_out", layer, t))
                row_stored()
                V.sem_inc(work_free, 1)
                emptied(v, job + ("vec", 0))
                last_read(V.tensor_tensor(work[:], pair[:], work[:], ALU.mult), fr, n)
                step(V.scalar_tensor_tensor(X(t), X(t), ALPHA, work[:], ALU.mult, ALU.add))
                statistics(t)
                normalised(job, t, X(t), 1, normed)

            def mod2(job):
                _, layer, t = job
                statistics(t)
                normalised(job, t, h_tok[:, tile_no[layer, t] % 2, :], 0, h_ready)

            def issue(ins):
                counts[dve_step.name] = counts.get(dve_step.name, 0) + 1
                ins.then_inc(dve_step, 1)
                return counts[dve_step.name]

            def top16(*searches):
                def turn(stage, vals, idxs, src, left):
                    if stage == 0:
                        return V.max(vals[:, 0:8], src)
                    if stage == 1:
                        return V.max_index(idxs[:, 0:8], vals[:, 0:8], src)
                    if stage == 2:
                        return V.match_replace(left, vals[:, 0:8], src, LOWEST)
                    if stage == 3:
                        return V.max(vals[:, 8:16], left)
                    return V.max_index(idxs[:, 8:16], vals[:, 8:16], left)

                made = [0] * len(searches)
                for stage in range(5):
                    for i, search in enumerate(searches):
                        if stage not in (0, 2):
                            v.wait_ge(dve_step, made[i])
                        made[i] = issue(turn(stage, *search))
                v.wait_ge(dve_step, made[-1])

            def topk(job):
                _, layer, t, h = job
                if h % 2 == 0:
                    emptied(v, ("query", layer, t, h // 2, "scores"))
                halves = [slice(p * TOPK, (p + 1) * TOPK) for p in range(2)]
                top16(*[(tv[:, halves[p]], tiu[:, halves[p]],
                         scores_sb[:, (h // 2) % 2, (2 * (h % 2) + p) * P:(2 * (h % 2) + p + 1) * P],
                         rest[:, p * P:(p + 1) * P]) for p in range(2)])
                if h % 2:
                    V.sem_inc(scores_free, 1)
                wide = [P, TOPK, TOPK]
                cands = view(cand, TOPK)
                issue(V.tensor_copy(tif, tiu[:]))
                step(V.tensor_tensor(cands, tv[:, 0:TOPK].unsqueeze(2).to_broadcast(wide),
                                     tv[:, TOPK:].unsqueeze(1).to_broadcast(wide), ALU.add))
                top16((bv[:, h * TOPK:(h + 1) * TOPK], bpu[:], cand, rest))
                issue(V.tensor_scalar(bij_u[:, 0:TOPK], bpu[:], 4, None, ALU.logical_shift_right))
                step(V.tensor_scalar(bij_u[:, TOPK:], bpu[:], 15, None, ALU.bitwise_and))
                step(V.tensor_copy(bij, bij_u[:]))
                onehots = (view(onehot, TOPK), cands)
                made = [0, 0]
                for p, oh in enumerate(onehots):
                    made[p] = issue(V.tensor_tensor(oh, bij[:, halves[p]].unsqueeze(2).to_broadcast(wide),
                                                    iota16[:].unsqueeze(1).to_broadcast(wide), ALU.is_equal))
                for p, oh in enumerate(onehots):
                    v.wait_ge(dve_step, made[p])
                    made[p] = issue(V.tensor_tensor(oh, oh, tif[:, halves[p]].unsqueeze(1).to_broadcast(wide), ALU.mult))
                for p, oh in enumerate(onehots):
                    v.wait_ge(dve_step, made[p])
                    made[p] = issue(V.tensor_reduce(e12[:, halves[p]], oh, AX.X, ALU.add))
                v.wait_ge(dve_step, made[1])
                step(V.scalar_tensor_tensor(idx_f, e12[:, 0:TOPK], float(NKEYS), e12[:, TOPK:], ALU.mult, ALU.add))
                idx = idx_tok[tile_no[layer, t] % 3]
                signal(V.tensor_copy(idx[:, h * TOPK:(h + 1) * TOPK], idx_f), idx_ready)

            def topk_end(job):
                b = tile_no[job[1:]] % 2
                wide = [P, PH, TOPK]
                hv, gv = view(bv[:], PH), view(gates[b][:], PH)
                signal(V.tensor_tensor(gv, hv, hv[:, :, 0:1].to_broadcast(wide), ALU.subtract), gate_sub)
                take("dve", v, gate_exp)
                step(V.tensor_reduce(gsum, gv, AX.X, ALU.add))
                step(V.reciprocal(gsum, gsum))
                step(V.tensor_tensor(gv, gv, gsum.unsqueeze(2).to_broadcast(wide), ALU.mult))

            do = dict(ada=ada, mod1=mod1, rope=rope, attn=attn, heads_out=heads_out, add_norm=add_norm, mod2=mod2,
                      topk=topk, topk_end=topk_end)

            def dot(tile, s, g=None):
                n, r = tile_no[tile], s % GROUP
                landed = 16 * (n * GROUPS + s // GROUP + 1)
                v.wait_ge(u_in[r], landed if g is None else g * 16 + landed)
                a = acts[:, s:s + 1] if g is None else acts[:, bass.ds(g * GROUP + s, 1)]
                V.scalar_tensor_tensor(u_rows[:, r, :], u_rows[:, r, :], 1.0, h_tok[:, n % 2, :], ALU.mult, ALU.mult,
                                       accum_out=a).then_inc(u_used, 1)

            V.sem_inc(u_used, GROUP)
            take("dve", v, cc_exp_done)
            step(V.tensor_scalar(silu_c[:], cc_exp, 1.0, None, ALU.add))
            step(V.reciprocal(silu_c[:], silu_c[:]))
            signal(V.tensor_tensor(silu_c[:], silu_c[:], cc, ALU.mult), silu_done)
            for job in start_jobs:
                if job == ("mod1", 0, CTX_TILES, 0):
                    v.wait_ge(const_in, 16 * 8)
                    v.wait_ge(ctx_in, 16)
                if job == ("mod1", 0, LAT_TILES, LAT_TILES[0]):
                    v.wait_ge(latents_in, 16)
                if job[0] in do:
                    do[job[0]](job)
            for u_tile, v_tile, slots in phases:
                if slots is None and u_tile is not None:
                    with v.Fori(0, GROUPS) as g:
                        for r in range(GROUP):
                            dot(u_tile, r, g)
                for s, jobs in enumerate(slots or []):
                    dot(u_tile, s)
                    for job in jobs:
                        if job[0] in do:
                            do[job[0]](job)
                if u_tile is not None:
                    v.wait_ge(u_used, GROUP + HK * (tile_no[u_tile] + 1))
                    V.sem_inc(acts_ready, 1)
                    b = tile_no[u_tile] % 2
                    take("dve", v, gelu_done)
                    signal(V.tensor_tensor(wts[b][:], acts[:], gates[b][:], ALU.mult), wts_ready)
                if v_tile is not None:
                    layer, t = v_tile
                    n = tile_no[v_tile] + 1
                    job = ("close",) + v_tile
                    row_stored()
                    V.sem_inc(work_free, 1)
                    v.wait_ge(v_used, GROUP + HK * n)
                    emptied(v, job + ("vec", 0))
                    signal(V.tensor_tensor(work[:], facc[:], work[:], ALU.mult), f_free)
                    step(V.scalar_tensor_tensor(X(t), X(t), ALPHA, work[:], ALU.mult, ALU.add))
                    statistics(t)
                    normalised(job, t, X(t), 1, x_done)

        @block.gpsimd
        def _(pool):
            need_u = es.enter_context(pool.register("need_u"))
            need_v = es.enter_context(pool.register("need_v"))
            need_staged = es.enter_context(pool.register("need_staged"))
            need_idx = es.enter_context(pool.register("need_idx"))
            pool.sem_inc(v_used, GROUP)
            pool.reg_mov(need_u, 1)
            pool.reg_mov(need_v, 1)
            pool.reg_mov(need_idx, 1)
            staged_before = 0
            pool.wait_ge(*chunk_freed[chunks[last_in[2]][0]])
            for u_tile, v_tile, _ in phases:
                if v_tile == tile_order[0]:
                    emptied(pool, ("project", 0, LAT_TILES, 3, 2))
                both = (u_tile is not None) + (v_tile is not None)
                pool.reg_mov(need_staged, staged_before + both)
                staged_before += both * GROUPS
                with pool.Fori(0, GROUPS // 2) as g:
                    if u_tile is not None:
                        pool.wait_ge(idx_ready, need_idx)
                        pool.reg_add(need_idx, need_idx, 1)
                    for half in range(2):
                        cols = slice(half * GROUP, (half + 1) * GROUP)
                        src = bass.ds(g * 2 * GROUP + half * GROUP, GROUP)
                        if u_tile is not None:
                            nc.gpsimd.tensor_copy(stage_u[:, cols], idx_tok[tile_no[u_tile] % 3][:, src]).then_inc(staged, 1)
                        if v_tile is not None:
                            nc.gpsimd.tensor_copy(stage_v[:, cols], idx_tok[tile_no[v_tile] % 3][:, src]).then_inc(staged, 1)
                        pool.wait_ge(staged, need_staged)
                        pool.reg_add(need_staged, need_staged, both)
                        for r in range(GROUP):
                            j = half * GROUP + r
                            if u_tile is not None:
                                pool.wait_ge(u_used, need_u)
                                pool.reg_add(need_u, need_u, 1)
                                pool.indirect_dma_start(
                                    u_rows[:, r, :], None, I[f"peer_u{u_tile[0]}"],
                                    bass.IndirectOffsetOnAxis(ap=stage_u[:, j:j + 1], axis=0)).then_inc(u_in[r], 16)
                            if v_tile is not None:
                                pool.wait_ge(v_used, need_v)
                                pool.reg_add(need_v, need_v, 1)
                                pool.indirect_dma_start(
                                    v_rows[:, r, :], None, I[f"peer_v{v_tile[0]}"],
                                    bass.IndirectOffsetOnAxis(ap=stage_v[:, j:j + 1], axis=0)).then_inc(v_in[r], 16)

        @block.sync
        def _(sp):
            sp.dma_start(cc, I["cc"]).then_inc(c_in, 16)
            rows_stored, loaded, biases = [0], [0], [0]

            def load(n):
                name, srcs = chunks[n]
                if before[n] >= 0:
                    sp.wait_ge(*chunk_freed[chunks[before[n]][0]])
                for src, col, rows in srcs:
                    sp.dma_start(slot_ap[chunk_slot[n]][0:rows, col:col + src.shape[-1]],
                                 src).then_inc(chunk_in[chunk_slot[n]], 16)

            def load_to(n):
                while loaded[0] < min(n, len(chunks)):
                    load(loaded[0])
                    loaded[0] += 1

            mod_rows = [job[:3] for job in all_jobs if job[0] == "ada" and job[3] == 1]

            def rows_needed(n):
                js = {"mod1": SCALE1, "add_norm": GATE1, "mod2": SCALE2, "close": GATE2}
                return max([0] + [mod_rows.index(("ada", name[1], js[name[0]])) + 1
                                  for name, _ in chunks[:n] if name[0] in js])

            def ahead(n):
                while loaded[0] < len(chunks) and before[loaded[0]] < n and rows_needed(loaded[0] + 1) <= rows_stored[0]:
                    load_to(loaded[0] + 1)

            def load_bias(t, h):
                if biases[0] >= 2:
                    sp.wait_ge(bias_free, biases[0] - 1)
                for a in range(2):
                    c = (NA_KR - 2 * (t - CT) - a) * GRID_W
                    sp.dma_start(bias[64 * a:64 * a + 64, biases[0] % 2, :],
                                 I["rpb"][h][:, c:c + NA_KR * GRID_W]).then_inc(bias_in[biases[0] % 2], 16)
                biases[0] += 1

            load_to(3)
            for dst, name in ((ident[:], "ident"), (chan_dft, "chan_dft"), (col_mask[:], "col_mask"),
                              (band_mask[:], "band_mask"), (rot[:], "rotate_half"), (iota16[:], "iota16")):
                sp.dma_start(dst, I[name]).then_inc(const_in, 16)
            sp.dma_start(sinks[:], bass.AP(I["gqa_sink"].tensor, 0, [[0, P], [1, QH]])).then_inc(const_in, 16)
            sp.dma_start(ones[0:1, :], I["ones"]).then_inc(const_in, 16)
            sp.dma_start(view(x_state[:, 0:CT * D], CT), I["ctx"].rearrange("(t p) d -> p t d", p=P)).then_inc(ctx_in, 16)
            for job, n in zip(in_order, chunks_by):
                load_to(n)
                if job[0] == "ada" and job[3] == 1:
                    sp.wait_ge(mod_row_ready, rows_stored[0] + 1)
                    dst = bass.AP(mod_dram.tensor, (job[1] * 6 + job[2]) * 2 * D, [[D, 2], [1, D]])
                    sp.dma_start(dst, mod_row).then_inc(mod_out, 16)
                    rows_stored[0] += 1
                    sp.wait_ge(mod_out, 16 * rows_stored[0])
                if job[0] == "attn" and job[1] == 0 and is_lat(job[2]):
                    if job[3] == 0:
                        load_bias(job[2], 0)
                    if job[3] + 1 < NA_HEADS:
                        load_bias(job[2], job[3] + 1)
                if job == ("mod1", 0, CTX_TILES, 0):
                    sp.dma_start(view(x_state[:, CT * D:], LT), I["x"].rearrange("(t p) d -> p t d", p=P)).then_inc(latents_in, 16)
                if job == ("mod1", 1, LAT_TILES[0:2], LAT_TILES[0]):
                    sp.wait_ge(idx_ready, PH * (tile_no[0, CT + LT - 1] + 1))
                    sp.dma_start(view(kv[:, 8704:9728], 2), I["rope"].rearrange("p (k n) -> p k n", k=2)).then_inc(rope_in, 16)
                ahead(n)
            for i in range(LT):
                sp.wait_ge(x_done, CT + LT + i + 1)
                sp.dma_start(out[i * P:(i + 1) * P, :], X(CT + i)).then_inc(out_done, 16)
            sp.wait_ge(out_done, 16 * LT)


def chunked(w, cols=512):
    n = w.shape[1] // cols
    return np.ascontiguousarray(w.reshape(KB, P, n, cols).transpose(2, 1, 0, 3).reshape(n, P, KB * cols))


def layout(inputs):
    a = {k: np.asarray(v) for k, v in inputs.items()}
    t = constants()
    t["x"] = a["x"][0]
    t["ctx"] = a["ctx"][0]
    t["cc"] = np.stack([a["c"][0].reshape(KB, P), a["c_ctx"].reshape(KB, P)], -1).transpose(1, 0, 2).reshape(P, KB * 2)
    t["ada_w"] = np.stack([chunked(a["ada_w"][l]) for l in range(DEPTH)])
    t["ada_b"] = a["ada_b"]
    t["post_g"], t["post_b"] = a["post_ln_g"], a["post_ln_b"]
    t["even_w_in"], t["even_w_out"] = chunked(a["even_w_in"][0]), chunked(a["even_w_out"][0])
    w = a["odd_w_in"][0]
    kw = w[:, QH * DH:(QH + KVH) * DH].reshape(D, KVH, 1, DH)
    kw = np.concatenate([kw, kw], 2).reshape(D, 512)
    t["odd_w_in"] = np.concatenate([chunked(w[:, :QH * DH]), chunked(kw)])
    t["odd_w_v"] = chunked(w[:, (QH + KVH) * DH:], 256)[0]
    t["odd_w_out"] = chunked(a["odd_w_out"][0])
    t["gqa_sink"] = a["gqa_sink"]
    rpb = a["na_rpb"][0]
    pad = np.zeros((NA_HEADS, 17, RPW), np.float32)
    c0 = GRID_W - NA_KC
    pad[:, 1:16, c0:c0 + 2 * NA_KC - 1] = rpb
    t["rpb"] = np.stack([pad[:, :, GRID_W - 1 - c:RPW - c] for c in range(GRID_W)], 1).reshape(NA_HEADS, GRID_W, -1)
    wq = np.stack([chunked(a["peer_w_q"][l]) for l in range(DEPTH)])
    sk = a["peer_sub_keys"].transpose(0, 4, 1, 2, 3).reshape(DEPTH, P, 4, 512).transpose(0, 2, 1, 3)
    t["peer_w_q"] = np.concatenate([wq, sk], -1)
    for l in range(DEPTH):
        t[f"peer_u{l}"], t[f"peer_v{l}"] = a["peer_u"][l], a["peer_v"][l]
    return {k: np.ascontiguousarray(v) for k, v in t.items()}


def kernel(**inputs):
    import concourse.bacc as bacc
    from concourse.bass_utils import run_bass_kernel_spmd

    nc = bacc.Bacc("TRN2", target_bir_lowering=False, num_devices=1)
    arrays = layout(inputs)
    I = {k: nc.dram_tensor("in_" + k, v.shape, F32, kind="ExternalInput").ap() for k, v in arrays.items()}
    out = nc.dram_tensor("out", (SEQ, D), F32, kind="ExternalOutput").ap()
    mod_dram = nc.dram_tensor("mod_rows", (DEPTH, 6, 2, D), F32, kind="Internal").ap()
    build(nc, I, out, mod_dram)
    r = run_bass_kernel_spmd(nc, [{"in_" + k: v for k, v in arrays.items()}], core_ids=[0])
    return r.results[0]["out"].reshape(1, SEQ, D)
```
